# Optimizing a Trainium2 kernel written in Bass

```python
import jax, jax.numpy as jnp
from jax import lax
import numpy as np

D_MODEL = 1024
BATCH = 1
SEQ = 512
DEPTH = 1

CHUNK = 64
RET_HEADS = 4
RET_QK_DIM = 256
RET_V_DIM = 256
RET_QK = RET_HEADS * RET_QK_DIM
RET_V = RET_HEADS * RET_V_DIM
POOL_WINDOWS = (2, 4, 8, 16)
POOL_GROUPS = 4
POOL_GROUP_DIM = 256
POOL_WIDTH = POOL_GROUPS * POOL_GROUP_DIM
N_BRANCH = 2
IN_WIDTH = 2 * RET_QK + 2 * RET_V + POOL_WIDTH + N_BRANCH * D_MODEL
D_FF = 2816
ROPE_BASE = 10000.0
NORM_EPS = 1e-6
FFN_RES_WEIGHT = 0.5


def rmsnorm(x, g):
    xf = x.astype(jnp.float32)
    y = xf * lax.rsqrt(jnp.mean(xf * xf, axis=-1, keepdims=True) + NORM_EPS)
    return (y * g.astype(jnp.float32)).astype(x.dtype)

def swiglu_ffn(x, w_in, w_out):
    gate, up = jnp.split(x @ w_in, 2, axis=-1)
    return (jax.nn.silu(gate) * up) @ w_out

def rotary(x):
    s, d = x.shape[1], x.shape[-1]
    half = d // 2
    inv_freq = ROPE_BASE ** (-jnp.arange(half, dtype=jnp.float32) / half)
    ang = jnp.arange(s, dtype=jnp.float32)[:, None] * inv_freq[None, :]
    cos = jnp.cos(ang)[None, :, None, :].astype(x.dtype)
    sin = jnp.sin(ang)[None, :, None, :].astype(x.dtype)
    x1, x2 = x[..., :half], x[..., half:]
    return jnp.concatenate([x1 * cos - x2 * sin, x1 * sin + x2 * cos], axis=-1)

def retention(q, k, v):
    b, s, h, dk = q.shape
    dv = v.shape[-1]
    nc = s // CHUNK
    log_gamma = jnp.log(1.0 - 2.0 ** (-5.0 - jnp.arange(h, dtype=jnp.float32)))
    idx = jnp.arange(CHUNK, dtype=jnp.float32)
    inner_decay = jnp.exp(log_gamma[:, None, None] * jnp.abs(idx[:, None] - idx[None, :]))
    q_decay = jnp.exp(log_gamma[None, :] * (idx[:, None] + 1.0))
    k_decay = jnp.exp(log_gamma[None, :] * (CHUNK - 1.0 - idx[:, None]))
    chunk_decay = jnp.exp(log_gamma * CHUNK)

    qc = q.reshape(b, nc, CHUNK, h, dk)
    kc = k.reshape(b, nc, CHUNK, h, dk)
    vc = v.reshape(b, nc, CHUNK, h, dv)

    scores = jnp.einsum("bnchd,bnshd->bnhcs", qc, kc) * inner_decay[None, None]
    inner = jnp.einsum("bnhcs,bnshe->bnche", scores, vc)

    def step(state, inp):
        q_i, k_i, v_i = inp
        cross = jnp.einsum("bchd,bhde->bche", q_i * q_decay[None, :, :, None], state)
        new_state = state * chunk_decay[None, :, None, None] + jnp.einsum(
            "bchd,bche->bhde", k_i * k_decay[None, :, :, None], v_i)
        return new_state, cross

    state0 = jnp.zeros((b, h, dk, dv), jnp.float32)
    xs = (qc.transpose(1, 0, 2, 3, 4), kc.transpose(1, 0, 2, 3, 4), vc.transpose(1, 0, 2, 3, 4))
    _, cross = lax.scan(step, state0, xs)
    out = inner + cross.transpose(1, 0, 2, 3, 4)
    return out.reshape(b, s, h, dv)

def multiscale_pool(p, w_group, scale):
    b, s, _ = p.shape
    pf = p.astype(jnp.float32).reshape(b, s, POOL_GROUPS, POOL_GROUP_DIM)
    cs = jnp.concatenate([jnp.zeros((b, 1, POOL_GROUPS, POOL_GROUP_DIM), jnp.float32),
                          jnp.cumsum(pf, axis=1)], axis=1)
    t = jnp.arange(s, dtype=jnp.float32)
    outs = []
    for g, w in enumerate(POOL_WINDOWS):
        cs_g = cs[:, :, g]
        shifted = jnp.pad(cs_g[:, : s + 1 - w], ((0, 0), (w - 1, 0), (0, 0)))
        count = jnp.minimum(t + 1.0, float(w))[None, :, None]
        outs.append((cs_g[:, 1:] - shifted) / count - pf[:, :, g])
    pooled = jnp.stack(outs, axis=2)
    mixed = jnp.einsum("bsgc,gcd->bsgd", pooled, w_group.astype(jnp.float32))
    return (mixed.reshape(b, s, POOL_WIDTH) * scale.astype(jnp.float32)).astype(p.dtype)

def first_inputs(seed: int = 0) -> dict:
    key = jax.random.key(seed)
    ks = jax.random.split(key, 20)
    f32 = jnp.float32

    def nrm(k, shape, fan_in):
        return jax.random.normal(k, shape, f32) * (fan_in ** -0.5)

    def gain(k, shape):
        return 1.0 + 0.02 * jax.random.normal(k, shape, f32)

    return {
        "x": jax.random.normal(ks[0], (BATCH, SEQ, D_MODEL), f32),
        "norm_ffn1": gain(ks[1], (DEPTH, D_MODEL)),
        "ffn1_w_in": nrm(ks[2], (DEPTH, D_MODEL, 2 * D_FF), D_MODEL),
        "ffn1_w_out": nrm(ks[3], (DEPTH, D_FF, D_MODEL), D_FF),
        "norm_mix": gain(ks[4], (DEPTH, D_MODEL)),
        "w_in": nrm(ks[5], (DEPTH, D_MODEL, IN_WIDTH), D_MODEL),
        "gate_bias": 0.02 * jax.random.normal(ks[6], (DEPTH, N_BRANCH, D_MODEL), f32),
        "pool_w": nrm(ks[7], (DEPTH, POOL_GROUPS, POOL_GROUP_DIM, POOL_GROUP_DIM), POOL_GROUP_DIM),
        "pool_scale": gain(ks[8], (DEPTH, POOL_WIDTH)),
        "w_ret_up": nrm(ks[9], (DEPTH, RET_V, D_MODEL), RET_V),
        "w_pool_up": nrm(ks[10], (DEPTH, POOL_WIDTH, D_MODEL), POOL_WIDTH),
        "w_out": nrm(ks[11], (DEPTH, D_MODEL, D_MODEL), D_MODEL),
        "norm_ffn2": gain(ks[12], (DEPTH, D_MODEL)),
        "ffn2_w_in": nrm(ks[13], (DEPTH, D_MODEL, 2 * D_FF), D_MODEL),
        "ffn2_w_out": nrm(ks[14], (DEPTH, D_FF, D_MODEL), D_FF),
        "norm_final": gain(ks[15], (D_MODEL,)),
    }

def first_block(x, norm_ffn1, ffn1_w_in, ffn1_w_out, norm_mix, w_in, gate_bias, pool_w,
              pool_scale, w_ret_up, w_pool_up, w_out, norm_ffn2, ffn2_w_in, ffn2_w_out,
              norm_final):
    b, s, _ = x.shape
    split_points = [RET_QK, 2 * RET_QK, 2 * RET_QK + RET_V, 2 * RET_QK + 2 * RET_V,
                    2 * RET_QK + 2 * RET_V + POOL_WIDTH]
    h = x
    for l in range(DEPTH):
        h = h + FFN_RES_WEIGHT * swiglu_ffn(rmsnorm(h, norm_ffn1[l]), ffn1_w_in[l], ffn1_w_out[l])

        u = rmsnorm(h, norm_mix[l])
        proj = u @ w_in[l]
        q, k, v, g_ret, p, gates = jnp.split(proj, split_points, axis=-1)
        q = rotary(q.reshape(b, s, RET_HEADS, RET_QK_DIM))
        k = rotary(k.reshape(b, s, RET_HEADS, RET_QK_DIM)) * (RET_QK_DIM ** -0.5)
        v = v.reshape(b, s, RET_HEADS, RET_V_DIM)
        ret = retention(q.astype(jnp.float32), k.astype(jnp.float32), v.astype(jnp.float32))
        ret = ret * lax.rsqrt(jnp.mean(ret * ret, axis=-1, keepdims=True) + NORM_EPS)
        ret = ret.reshape(b, s, RET_V).astype(proj.dtype) * jax.nn.silu(g_ret)

        pool_out = multiscale_pool(p, pool_w[l], pool_scale[l])

        gate = jax.nn.sigmoid(gates.reshape(b, s, N_BRANCH, D_MODEL) + gate_bias[l])
        merged = gate[:, :, 0] * (ret @ w_ret_up[l]) + gate[:, :, 1] * (pool_out @ w_pool_up[l])
        h = h + merged @ w_out[l]

        h = h + FFN_RES_WEIGHT * swiglu_ffn(rmsnorm(h, norm_ffn2[l]), ffn2_w_in[l], ffn2_w_out[l])
    return rmsnorm(h, norm_final)


D_MIX = D_MODEL
D_CONV = D_MIX // 2
CONV_GROUPS = 8
CONV_GROUP_DIM = D_CONV // CONV_GROUPS
CONV_WIDTH = 3
GDN_HEADS = 4
GDN_HEAD_DIM = (D_MIX - D_CONV) // GDN_HEADS
GDN_WIDTH = GDN_HEADS * GDN_HEAD_DIM
GDN_CONV_WIDTH = 4
GDN_CHUNK = 64
D_IN_PROJ = 3 * D_CONV + 4 * GDN_WIDTH + 2 * GDN_HEADS


def rmsnorm_2(x, w, eps=NORM_EPS):
    xf = x.astype(jnp.float32)
    y = xf * lax.rsqrt(jnp.mean(xf * xf, axis=-1, keepdims=True) + eps)
    return (y * w.astype(jnp.float32)).astype(x.dtype)

def l2norm(x, eps=NORM_EPS):
    return x * lax.rsqrt(jnp.sum(x * x, axis=-1, keepdims=True) + eps)

def swiglu_ffn_2(x, w_in, w_out):
    gate, up = jnp.split(x @ w_in, 2, axis=-1)
    return (jax.nn.silu(gate) * up) @ w_out

def causal_depthwise_conv(x, w):
    K, C = w.shape
    return lax.conv_general_dilated(
        x, w[:, None, :].astype(x.dtype), window_strides=(1,), padding=[(K - 1, 0)],
        dimension_numbers=('NWC', 'WIO', 'NWC'), feature_group_count=C)

def short_conv_mixer(b_gate, c_gate, h, conv_w, out_gain):
    y = b_gate * causal_depthwise_conv(c_gate * h, conv_w)
    bsz, t, _ = y.shape
    y = rmsnorm_2(y.reshape(bsz, t, CONV_GROUPS, CONV_GROUP_DIM),
                out_gain.reshape(CONV_GROUPS, CONV_GROUP_DIM))
    return y.reshape(bsz, t, D_CONV)

def gated_delta_rule_chunked(q, k, v, g, beta):
    bsz, t, nh, dk = q.shape
    dv = v.shape[-1]
    c = GDN_CHUNK
    n = t // c
    q = q * (dk ** -0.5)
    to_chunks = lambda a: a.reshape(bsz, n, c, nh, a.shape[-1]).transpose(0, 3, 1, 2, 4)
    q, k, v = to_chunks(q), to_chunks(k), to_chunks(v)
    beta = beta.reshape(bsz, n, c, nh).transpose(0, 3, 1, 2)
    g = jnp.cumsum(g.reshape(bsz, n, c, nh).transpose(0, 3, 1, 2), axis=-1)
    k_beta = k * beta[..., None]
    v_beta = v * beta[..., None]
    causal = jnp.tril(jnp.ones((c, c), dtype=bool))
    strict = jnp.tril(jnp.ones((c, c), dtype=bool), -1)
    gdiff = g[..., :, None] - g[..., None, :]
    decay = jnp.exp(jnp.where(causal, gdiff, -jnp.inf))
    lower = jnp.where(strict, jnp.einsum('bhncd,bhnsd->bhncs', k_beta, k) * decay, 0.0)
    rhs = jnp.concatenate([v_beta, k_beta * jnp.exp(g)[..., None]], axis=-1)
    sol = lax.linalg.triangular_solve(lower, rhs, left_side=True, lower=True, unit_diagonal=True)
    u, w = sol[..., :dv], sol[..., dv:]
    attn_intra = jnp.where(causal, jnp.einsum('bhncd,bhnsd->bhncs', q, k) * decay, 0.0)
    q_dec = q * jnp.exp(g)[..., None]
    k_dec = k * jnp.exp(g[..., -1:] - g)[..., None]
    g_last = jnp.exp(g[..., -1])
    xs = tuple(jnp.moveaxis(a, 2, 0) for a in (q_dec, k_dec, u, w, attn_intra, g_last))

    def step(state, inp):
        q_c, k_c, u_c, w_c, a_c, gl = inp
        v_new = u_c - jnp.einsum('bhck,bhkv->bhcv', w_c, state)
        o_c = jnp.einsum('bhck,bhkv->bhcv', q_c, state) + jnp.einsum('bhcs,bhsv->bhcv', a_c, v_new)
        state = state * gl[..., None, None] + jnp.einsum('bhck,bhcv->bhkv', k_c, v_new)
        return state, o_c

    s0 = jnp.zeros((bsz, nh, dk, dv), jnp.float32)
    _, o = lax.scan(step, s0, xs)
    return o.transpose(1, 0, 3, 2, 4).reshape(bsz, t, nh, dv)

def gated_deltanet_mixer(q, k, v, z, b, a, conv_w, A_log, dt_bias, norm_w):
    bsz, t, _ = q.shape
    qkv = jax.nn.silu(causal_depthwise_conv(jnp.concatenate([q, k, v], axis=-1), conv_w))
    q, k, v = jnp.split(qkv.astype(jnp.float32), 3, axis=-1)
    heads = lambda a_: a_.reshape(bsz, t, GDN_HEADS, GDN_HEAD_DIM)
    q, k, v = l2norm(heads(q)), l2norm(heads(k)), heads(v)
    beta = jax.nn.sigmoid(b.astype(jnp.float32))
    g = -jnp.exp(A_log.astype(jnp.float32)) * jax.nn.softplus(a.astype(jnp.float32) + dt_bias.astype(jnp.float32))
    o = gated_delta_rule_chunked(q, k, v, g, beta)
    o = rmsnorm_2(o, norm_w) * jax.nn.silu(heads(z).astype(jnp.float32))
    return o.reshape(bsz, t, GDN_WIDTH).astype(z.dtype)

def second_inputs(seed: int = 0) -> dict:
    key = jax.random.key(seed)
    ks = jax.random.split(key, 20)
    nrm = lambda k_, shape, fan_in: jax.random.normal(k_, shape, jnp.float32) * (fan_in ** -0.5)
    gain = lambda k_, shape: 1.0 + 0.05 * jax.random.normal(k_, shape, jnp.float32)
    L = DEPTH
    return {
        'x': jax.random.normal(ks[0], (BATCH, SEQ, D_MODEL), jnp.float32),
        'ffn1_norm': gain(ks[1], (L, D_MODEL)),
        'ffn1_w_in': nrm(ks[2], (L, D_MODEL, 2 * D_FF), D_MODEL),
        'ffn1_w_out': nrm(ks[3], (L, D_FF, D_MODEL), D_FF),
        'mix_norm': gain(ks[4], (L, D_MODEL)),
        'w_mix_in': nrm(ks[5], (L, D_MODEL, D_IN_PROJ), D_MODEL),
        'conv_short_w': nrm(ks[6], (L, CONV_WIDTH, D_CONV), CONV_WIDTH),
        'conv_out_norm': gain(ks[7], (L, D_CONV)),
        'gdn_conv_w': nrm(ks[8], (L, GDN_CONV_WIDTH, 3 * GDN_WIDTH), GDN_CONV_WIDTH),
        'gdn_A_log': jnp.log(jax.random.uniform(ks[9], (L, GDN_HEADS), jnp.float32, 1.0, 16.0)),
        'gdn_dt_bias': 1.0 + 0.1 * jax.random.normal(ks[10], (L, GDN_HEADS), jnp.float32),
        'gdn_out_norm': gain(ks[11], (L, GDN_HEAD_DIM)),
        'w_mix_out': nrm(ks[12], (L, D_MIX, D_MODEL), D_MIX),
        'ffn2_norm': gain(ks[13], (L, D_MODEL)),
        'ffn2_w_in': nrm(ks[14], (L, D_MODEL, 2 * D_FF), D_MODEL),
        'ffn2_w_out': nrm(ks[15], (L, D_FF, D_MODEL), D_FF),
        'final_norm': gain(ks[16], (D_MODEL,)),
    }

def second_block(x, ffn1_norm, ffn1_w_in, ffn1_w_out, mix_norm, w_mix_in, conv_short_w, conv_out_norm,
              gdn_conv_w, gdn_A_log, gdn_dt_bias, gdn_out_norm, w_mix_out, ffn2_norm, ffn2_w_in,
              ffn2_w_out, final_norm):
    sizes = [D_CONV, D_CONV, D_CONV, GDN_WIDTH, GDN_WIDTH, GDN_WIDTH, GDN_WIDTH, GDN_HEADS, GDN_HEADS]
    splits = np.cumsum(sizes)[:-1].tolist()
    h = x
    for layer in range(DEPTH):
        h = h + 0.5 * swiglu_ffn_2(rmsnorm_2(h, ffn1_norm[layer]), ffn1_w_in[layer], ffn1_w_out[layer])
        u = rmsnorm_2(h, mix_norm[layer]) @ w_mix_in[layer]
        cb, cc, ch, gq, gk, gv, gz, gb, ga = jnp.split(u, splits, axis=-1)
        y_conv = short_conv_mixer(cb, cc, ch, conv_short_w[layer], conv_out_norm[layer])
        y_gdn = gated_deltanet_mixer(gq, gk, gv, gz, gb, ga, gdn_conv_w[layer], gdn_A_log[layer],
                                     gdn_dt_bias[layer], gdn_out_norm[layer])
        h = h + jnp.concatenate([y_conv, y_gdn], axis=-1) @ w_mix_out[layer]
        h = h + 0.5 * swiglu_ffn_2(rmsnorm_2(h, ffn2_norm[layer]), ffn2_w_in[layer], ffn2_w_out[layer])
    return rmsnorm_2(h, final_norm)


def setup_inputs(seed=0):
    out = dict(first_inputs(seed))
    for name, value in second_inputs(seed + 1).items():
        if name != "x":
            out[name + "_2"] = value
    return out


def reference(
    x, norm_ffn1, ffn1_w_in, ffn1_w_out, norm_mix, w_in, gate_bias, pool_w, pool_scale,
    w_ret_up, w_pool_up, w_out, norm_ffn2, ffn2_w_in, ffn2_w_out, norm_final, ffn1_norm_2,
    ffn1_w_in_2, ffn1_w_out_2, mix_norm_2, w_mix_in_2, conv_short_w_2, conv_out_norm_2,
    gdn_conv_w_2, gdn_A_log_2, gdn_dt_bias_2, gdn_out_norm_2, w_mix_out_2, ffn2_norm_2,
    ffn2_w_in_2, ffn2_w_out_2, final_norm_2,
):
    x = first_block(
        x, norm_ffn1, ffn1_w_in, ffn1_w_out, norm_mix, w_in, gate_bias, pool_w, pool_scale,
        w_ret_up, w_pool_up, w_out, norm_ffn2, ffn2_w_in, ffn2_w_out, norm_final,
    )
    return second_block(
        x, ffn1_norm_2, ffn1_w_in_2, ffn1_w_out_2, mix_norm_2, w_mix_in_2, conv_short_w_2,
        conv_out_norm_2, gdn_conv_w_2, gdn_A_log_2, gdn_dt_bias_2, gdn_out_norm_2, w_mix_out_2,
        ffn2_norm_2, ffn2_w_in_2, ffn2_w_out_2, final_norm_2,
    )


_drawn_inputs = setup_inputs


def setup_inputs(seed=0):
    import zlib

    import numpy as np

    out = dict(_drawn_inputs(seed))
    spreads = {}
    factors = {'norm_ffn1': 3.792,
     'norm_mix': 2.679,
     'gate_bias': 8.0,
     'pool_scale': 4.948,
     'norm_ffn2': 5.662,
     'gdn_dt_bias_2': 64.0,
     'gdn_out_norm_2': 3.844,
     'ffn2_norm_2': 3.477,
     'gdn_A_log_2': 8.0}
    for name, (base, spread) in spreads.items():
        noise = np.random.default_rng([zlib.crc32(name.encode()), seed]).standard_normal(out[name].shape)
        drawn = base * np.exp(spread * noise) if base else spread * noise
        out[name] = __import__('jax').numpy.asarray(drawn.astype(out[name].dtype))
    for name, factor in factors.items():
        out[name] = (out[name] * factor).astype(out[name].dtype)
    return out
```

```python
from contextlib import ExitStack

import numpy as np

import concourse.bass as bass
from concourse import mybir

F32 = mybir.dt.float32
F32R = mybir.dt.float32r
ALU = mybir.AluOpType
ACT = mybir.ActivationFunctionType

P = 128
S = 512
D = 1024
KD = D // P
FF = 2816
KF = FF // P
EPS = 1e-6
NT = S // P
HEADS = 4
DK = 256
W2 = 128
POOL = (2, 4, 8, 16)
PADP = 16
SLOTS = 4
LIMIT = 211968
LEAD = 2
TILES = 8

PHASES = [("ffn0_in", 2 * KF), ("ffn0_out", 3 * KD), ("pool_in", 8), ("v", 8), ("pool_mix", 4),
          ("pool_up", 16), ("heads", 24), ("ret_up", 16), ("mix_out", 8), ("ffn1_in", 2 * KF), ("ffn1_out", 3 * KD),
          ("ffn2_in", 2 * KF), ("ffn2_out", 3 * KD), ("gdn_qkv", 12), ("gdn_gate", 4), ("conv", 12),
          ("mix2_out", 8), ("ffn3_in", 2 * KF), ("ffn3_out", 3 * KD)]
FIRST, NB = {}, 0
for _name, _count in PHASES:
    FIRST[_name] = NB
    NB += _count
OUT0, _n = {}, 0
for _name, _count in PHASES:
    OUT0[_name] = _n
    _n += {"ffn0_out": 8, "ffn1_out": 8, "ffn2_out": 8, "ffn3_out": 8, "pool_mix": 8}.get(_name, _count)

VEC = {}
NV = 0
for _name, _n2 in [("norm_ffn1", 8), ("norm_mix", 8), ("gate_bias", 16), ("pool_scale", 8), ("norm_ffn2", 8),
                   ("norm_final", 8), ("ffn1_norm_2", 8), ("mix_norm_2", 8), ("conv_short_w_2", 12),
                   ("conv_out_norm_2", 4), ("gdn_conv_w_2", 48), ("gdn_out_norm_2", 1), ("ffn2_norm_2", 8),
                   ("final_norm_2", 8), ("A_log", 4), ("dt_bias", 4), ("w_ab", 64)]:
    VEC[_name] = NV
    NV += _n2
C_ONES, C_IDENT, C_EPS, C_ONE, C_EDGE = 0, 128, 256, 257, 258
NC0 = C_EDGE + 4 * PADP
C_COS, C_SIN, C_DECAY = 0, S, 2 * S
NC1 = 6 * S
C_TRI, C_CAUSAL, C_STRICT, C_GROUP, C_LEVEL = 0, 128, 256, 384, 512
LEVELS = 7
NC2 = C_LEVEL + (LEVELS + 1) * P


def build(nc, weights, x_t, vectors, const0, const1, const2, out):
    with ExitStack() as ctx:
        top = [0]

        def sbuf_at(name, offset, shape, dt=F32):
            with ExitStack() as c:
                if offset:
                    c.enter_context(nc.sbuf_tensor(name + "_below", [P, offset // 4], F32))
                t = c.enter_context(nc.sbuf_tensor(name, [P] + list(shape), dt))
            size = 4 * int(np.prod(shape))
            top[0] = max(top[0], offset + size)
            return t, offset + (size + 31) // 32 * 32

        def sem(name):
            return ctx.enter_context(nc.semaphore(name))

        at = 0
        h, at = sbuf_at("h", at, [KD, S])
        x_hi, at = sbuf_at("x_hi", at, [KD, S], F32R)
        x_lo, at = sbuf_at("x_lo", at, [KD, S], F32R)
        w_raw, _ = sbuf_at("w_raw", at, [SLOTS, TILES * P])
        w_lo, at = sbuf_at("w_lo", at, [SLOTS, TILES * P], F32R)
        w_hi, at = sbuf_at("w_hi", at, [SLOTS, TILES * P], F32R)
        square, at = sbuf_at("square", at, [2, S])
        sumsq, at = sbuf_at("sumsq", at, [S])
        root, at = sbuf_at("root", at, [S])
        rstd, at = sbuf_at("rstd", at, [S])
        vec, at = sbuf_at("vec", at, [NV])
        cst, at = sbuf_at("cst", at, [NC0])
        rtok, at = sbuf_at("rtok", at, [8])
        arena = at
        hid_hi, a = sbuf_at("hid_hi", arena, [KF, S], F32R)
        hid_lo, a = sbuf_at("hid_lo", a, [KF, S], F32R)
        f_gate, a = sbuf_at("f_gate", a, [2, S])
        f_sig, a = sbuf_at("f_sig", a, [2, S])
        f_mul, a = sbuf_at("f_mul", a, [2, S])
        f_hid, a = sbuf_at("f_hid", a, [2, S])
        sumsq2, b = sbuf_at("sumsq2", a, [S])
        r_one, b = sbuf_at("r_one", b, [S])
        square2, b = sbuf_at("square2", b, [2, S])
        assert b <= LIMIT
        pooled_hi, half = sbuf_at("pooled_hi", arena, [KD, S], F32R)
        pooled_lo, b = sbuf_at("pooled_lo", half, [KD, S], F32R)
        merged1, half = sbuf_at("merged1", arena, [KD, S])
        qk, a = sbuf_at("qk", half, [4, S])
        r_raw, a = sbuf_at("r_raw", a, [2, S])
        silu_g, a = sbuf_at("silu_g", a, [2, S])
        assert a == b
        merged_hi, a = sbuf_at("merged_hi", half, [KD, S], F32R)
        merged_lo, b = sbuf_at("merged_lo", a, [KD, S], F32R)
        v_tok, a = sbuf_at("v_tok", a, [NT, D])
        mix_hi, a = sbuf_at("mix_hi", a, [KD, S], F32R)
        mix_lo, a = sbuf_at("mix_lo", a, [KD, S], F32R)
        p_raw, b = sbuf_at("p_raw", a, [2, PADP + S])
        p_sum, b = sbuf_at("p_sum", b, [2, PADP + S])
        p_out, pool_end = sbuf_at("p_out", b, [2, S])
        scored, b = sbuf_at("scored", a, [S + 384 + 256 + 128])
        rot, b = sbuf_at("rot", b, [4, S])
        m_tmp, b = sbuf_at("m_tmp", max(pool_end, b), [2, S])
        m_sig, b = sbuf_at("m_sig", b, [2, S])
        k1c, b = sbuf_at("k1c", b, [NC1])
        final_hi, a = sbuf_at("final_hi", arena, [4, S], F32R)
        final_lo, a = sbuf_at("final_lo", a, [4, S], F32R)
        k2c, a = sbuf_at("k2c", a, [NC2])
        q_t, a = sbuf_at("q_t", a, [HEADS, S])
        v_tk, a = sbuf_at("v_tk", a, [NT, HEADS, W2])
        o_t, a = sbuf_at("o_t", a, [HEADS, S])
        z_t, a = sbuf_at("z_t", a, [HEADS, S])
        y_inv_t, a = sbuf_at("y_inv_t", a, [NT, HEADS, P])
        gdn_hi, _ = sbuf_at("gdn_hi", a, [HEADS, S], F32R)
        k_t, a = sbuf_at("k_t", a, [HEADS, S])
        gdn_lo, _ = sbuf_at("gdn_lo", a, [HEADS, S], F32R)
        k_tk, a = sbuf_at("k_tk", a, [NT, HEADS, W2])
        at_t, a = sbuf_at("at_t", a, [NT, HEADS, P])
        small, a = sbuf_at("small", a, [16 * 16])
        scratch = a
        wab_hi, a = sbuf_at("wab_hi", a, [KD, 8], F32R)
        wab_lo, a = sbuf_at("wab_lo", a, [KD, 8], F32R)
        scratch = a
        c_raw, a = sbuf_at("c_raw", scratch, [2, 4 + S])
        c_acc, a = sbuf_at("c_acc", a, [2, S])
        c_sig, a = sbuf_at("c_sig", a, [2, S])
        c_gate, a = sbuf_at("c_gate", a, [2, S])
        c_y, a = sbuf_at("c_y", a, [2, S])
        state, a = sbuf_at("state", a, [HEADS, W2])
        u_state, a = sbuf_at("u_state", a, [HEADS, W2])
        d_g, a = sbuf_at("d_g", scratch, [HEADS, P])
        d_exp, a = sbuf_at("d_exp", a, [HEADS, P])
        d_row, a = sbuf_at("d_row", a, [HEADS, P])
        d_l, a = sbuf_at("d_l", a, [HEADS, P])
        d_a, a = sbuf_at("d_a", a, [HEADS, P])
        d_lt, a = sbuf_at("d_lt", a, [HEADS, P])
        d_x, a = sbuf_at("d_x", a, [HEADS, P])
        d_p, a = sbuf_at("d_p", a, [HEADS, P])
        d_m, a = sbuf_at("d_m", a, [HEADS, P])
        d_t, a = sbuf_at("d_t", a, [HEADS, P])
        u_r, _ = sbuf_at("u_r", scratch, [HEADS, P])
        u_v, _ = sbuf_at("u_v", scratch + 2048, [HEADS, P])
        u_t, _ = sbuf_at("u_t", scratch + 4096, [HEADS, P])

        acc = [ctx.enter_context(nc.psum_tensor(f"acc{i}", [P, S], F32)) for i in range(4)]
        sums = ctx.enter_context(nc.psum_tensor("sums", [P, S], F32))
        mixb = [ctx.enter_context(nc.psum_tensor(f"mixb{i}", [P, S], F32)) for i in range(3)]

        ones, ident = cst[:, C_ONES:C_ONES + P], cst[:, C_IDENT:C_IDENT + P]
        eps, one = cst[:, C_EPS:C_EPS + 1], cst[:, C_ONE:C_ONE + 1]

        def vcol(name, j, n=1):
            return vec[:, VEC[name] + j:VEC[name] + j + n]

        SMALL = ["g", "beta", "z", "nz", "u", "w", "lnw", "eq", "d", "cum", "total", "e_cum", "e_left", "e_total",
                 "neg_a", "ab4"]

        def sm(name):
            i = 16 * SMALL.index(name)
            return small[:, i:i + 16]

        def per_head(name, c):
            i = 16 * SMALL.index(name) + 4 * c
            return small[:, i:i + 4].unsqueeze(2).to_broadcast([P, HEADS, P])

        def over_heads(column):
            return k2c[:, column:column + P].unsqueeze(1).to_broadcast([P, HEADS, P])

        ident_h = cst[:, C_IDENT:C_IDENT + P].unsqueeze(1).to_broadcast([P, HEADS, P])

        def bank_h(bank):
            return bank[:, :].rearrange("p (h n) -> p h n", h=HEADS)

        def scored_at(i):
            return i * S - P * (i * (i - 1) // 2)

        x_loaded = [sem(f"x_loaded{i}") for i in range(4)]
        tables_loaded = sem("tables_loaded")
        k1_loaded = sem("k1_loaded")
        k2_loaded = sem("k2_loaded")
        loaded = [sem(f"loaded{i}") for i in range(SLOTS)]
        hi_split = sem("hi_split")
        lo_split = sem("lo_split")
        block_done = sem("block_done")
        drained = sem("drained")
        sq_done = sem("sq_done")
        sq_summed = sem("sq_summed")
        x_hi_done = sem("x_hi_done")
        x_done = sem("x_done")
        summed = sem("summed")
        rooted = sem("rooted")
        inverted = sem("inverted")
        f_sig_done = sem("f_sig_done")
        f_step = sem("f_step")
        f_mul_done = sem("f_mul_done")
        hid_hi_done = sem("hid_hi_done")
        hid_done = sem("hid_done")
        chained = sem("chained")
        sq2_done = sem("sq2_done")
        sq2_summed = sem("sq2_summed")
        h_chain = sem("h_chain")
        h_final = sem("h_final")
        zeroed = sem("zeroed")
        dve_step = sem("dve_step")
        pool_step = sem("pool_step")
        act_step = sem("act_step")
        pool_out_done = sem("pool_out_done")
        pooled_hi_done = sem("pooled_hi_done")
        pooled_done = sem("pooled_done")
        m_sig_done = sem("m_sig_done")
        mix_hi_done = sem("mix_hi_done")
        mix_done = sem("mix_done")
        rotated = sem("rotated")
        g_ready = sem("g_ready")
        scores_done = sem("scores_done")
        weighted = sem("weighted")
        av_done = sem("av_done")
        ret_copied = sem("ret_copied")
        ret_sq = sem("ret_sq")
        ret_normed = sem("ret_normed")
        ret_gated = sem("ret_gated")
        merged_sum = sem("merged_sum")
        merged_hi_done = sem("merged_hi_done")
        merged_done = sem("merged_done")
        y_ready = sem("y_ready")
        stored = sem("stored")
        ab_done = sem("ab_done")
        wab_split = sem("wab_split")
        wab_hi_done = sem("wab_hi_done")
        ab_ready = sem("ab_ready")
        ab_act = sem("ab_act")
        g_cum = sem("g_cum")
        conv_done = sem("conv_done")
        conv_sig = sem("conv_sig")
        conv_act = sem("conv_act")
        l2_sq = sem("l2_sq")
        l2_done = sem("l2_done")
        turned = sem("turned")
        turned_copied = sem("turned_copied")
        c_gated = sem("c_gated")
        c_conv = sem("c_conv")
        c_prod = sem("c_prod")
        c_sq = sem("c_sq")
        c_normed = sem("c_normed")
        c_hi = sem("c_hi")
        c_split = sem("c_split")
        z_sig = sem("z_sig")
        z_ready = sem("z_ready")
        row_in = sem("row_in")
        row_done = sem("row_done")
        diff_done = sem("diff_done")
        exp_done = sem("exp_done")
        decay_ready = sem("decay_ready")
        kk_done = sem("kk_done")
        ld_done = sem("ld_done")
        l_done = sem("l_done")
        lt_turned = sem("lt_turned")
        lt_copied = sem("lt_copied")
        x0_done = sem("x0_done")
        m_ready = sem("m_ready")
        p_done = sem("p_done")
        p_copied = sem("p_copied")
        xp_done = sem("xp_done")
        x_level = sem("x_level")
        q_dec = sem("q_dec")
        ks_done = sem("ks_done")
        r_done = sem("r_done")
        vn_done = sem("vn_done")
        vn_copied = sem("vn_copied")
        os_done = sem("os_done")
        o_copied = sem("o_copied")
        state_done = sem("state_done")
        o_sq = sem("o_sq")
        o_normed = sem("o_normed")
        o_gated = sem("o_gated")
        o_hi = sem("o_hi")
        o_split = sem("o_split")

        def counter(engine, semaphore):
            count = [0]

            def step(instruction):
                count[0] += 1
                instruction.then_inc(semaphore, 1)
                engine.wait_ge(semaphore, count[0])
            return step

        SUM = {}
        for name in (["norm0", "norm1", "token1"] + [f"ret{i}" for i in range(HEADS)] + ["norm2", "norm3", "norm3b",
                     "norm4", "token4"] + [f"l2_{i}" for i in range(2 * HEADS)] + [f"conv{i}" for i in range(4)]
                     + [f"out{i}" for i in range(HEADS)] + ["norm5", "norm6"]):
            SUM[name] = len(SUM)
        NORM = [("norm_ffn1", None, None), ("norm_mix", "ffn0_out", 0.5), ("norm_ffn2", "mix_out", 1.0),
                ("ffn1_norm_2", "ffn1_out", 0.5), ("mix_norm_2", "ffn2_out", 0.5),
                ("ffn2_norm_2", "mix2_out", 1.0), (None, "ffn3_out", 0.5)]
        FFN_NORM = [0, 2, 3, 5]

        block = ctx.enter_context(nc.Block())

        @block.sync
        def _(sp):
            sp.dma_start(cst[:, :], const0).then_inc(tables_loaded, 16)
            sp.dma_start(vec[:, :], vectors).then_inc(tables_loaded, 16)
            for i in range(4):
                sp.dma_start(h[:, 2 * i:2 * i + 2, :], x_t[:, 2 * i:2 * i + 2, :]).then_inc(x_loaded[i], 16)
                sp.dma_start(w_raw[:, i, :], weights[i]).then_inc(loaded[i], 16)
            with sp.Fori(1, NB // SLOTS) as turn:
                for slot in range(SLOTS):
                    sp.wait_ge(block_done, SLOTS * turn + (slot - SLOTS + 1))
                    sp.dma_start(w_raw[:, slot, :], weights[SLOTS * turn + slot]).then_inc(loaded[slot], 16)
            for m in range(KD):
                sp.wait_ge(y_ready, m + 1)
                sp.dma_start(out[:, m, :], h[:, m, :]).then_inc(stored, 16)
            sp.wait_ge(stored, 16 * KD)

        @block.tensor
        def _(pe):
            def product(slot, j, bank, hi, lo, start, stop):
                w = slice(j * P, (j + 1) * P)
                pe.matmul(bank, w_hi[:, slot, w], hi, start=start, stop=False)
                pe.matmul(bank, w_hi[:, slot, w], lo, start=False, stop=False)
                return pe.matmul(bank, w_lo[:, slot, w], hi, start=False, stop=stop)

            def take_block(n):
                pe.wait_ge(lo_split, n + 1)

            def take_bank(a):
                if a >= 4:
                    pe.wait_ge(drained, a - 3)

            def dense(n, a, hi, lo):
                take_block(n)
                take_bank(a)
                for k in range(KD):
                    last = product(n % SLOTS, k, acc[a % 4][:, :], hi[:, k, :], lo[:, k, :], k == 0, k == KD - 1)
                last.then_inc(block_done, 1)

            def sum_over_features(name, source, wait, value, left=ones):
                n = SUM[name]
                pe.wait_ge(wait, value)
                if n:
                    pe.wait_ge(rooted, n)
                pe.matmul(sums[:, :], left, source, start=True, stop=True).then_inc(summed, 1)

            def token_sums(name):
                pe.wait_ge(rooted, SUM[name])
                for t in range(NT):
                    last = pe.matmul(sums[:, t:t + 1], sumsq[:, t * P:(t + 1) * P], ones[:, 0:1], start=True, stop=True)
                last.then_inc(summed, 1)

            def ffn(f):
                first, out0 = FIRST[f"ffn{f}_in"], OUT0[f"ffn{f}_in"]
                r = FFN_NORM[f]
                for k in range(KD):
                    pe.wait_ge(x_done, KD * r + k + 1)
                    if k == 0:
                        take_block(first)
                        take_bank(out0)
                    last = product(0, k, acc[0][:, :], x_hi[:, k, :], x_lo[:, k, :], k == 0, k == KD - 1)
                last.then_inc(block_done, 1)
                sum_over_features(f"norm{r}", sumsq[:, :], sq_summed, KD * (r + 1))
                if f == 2:
                    sum_over_features("norm3b", sumsq2[:, :], sq2_summed, KD)
                for n in range(first + 1, first + SLOTS):
                    dense(n, out0 + n - first, x_hi, x_lo)
                with pe.Fori(1, 2 * KF // SLOTS) as i:
                    for b in range(SLOTS):
                        pe.wait_ge(lo_split, SLOTS * i + (first + b + 1))
                        pe.wait_ge(drained, SLOTS * i + (out0 + b - 3))
                        for k in range(KD):
                            last = product(b, k, acc[b][:, :], x_hi[:, k, :], x_lo[:, k, :], k == 0, k == KD - 1)
                        last.then_inc(block_done, 1)
                first, out0 = FIRST[f"ffn{f}_out"], OUT0[f"ffn{f}_out"]
                with pe.Fori(0, KD // 4) as i:
                    for m in range(4):
                        pe.wait_ge(drained, 4 * i + (out0 + m - 3))
                        for part in range(3):
                            b = 3 * m + part
                            pe.wait_ge(lo_split, 12 * i + (first + b + 1))
                            upto = min(KF, TILES * (part + 1))
                            pe.wait_ge(hid_done, KF * f + upto)
                            for k in range(TILES * part, upto):
                                last = product(b % SLOTS, k - TILES * part, acc[m][:, :], hid_hi[:, k, :],
                                               hid_lo[:, k, :], k == 0, k == KF - 1)
                            last.then_inc(block_done, 1)

            def gated_mix(phase, hi, lo, wait, value):
                first, out0 = FIRST[phase], OUT0[phase]
                for m in range(KD):
                    dense(first + 2 * m, out0 + 2 * m, x_hi, x_lo)
                    if m == 0:
                        if phase == "ret_up":
                            sum_over_features(f"ret{HEADS - 1}", sumsq[:, :], ret_sq, HEADS)
                        pe.wait_ge(wait, value)
                    dense(first + 2 * m + 1, out0 + 2 * m + 1, hi, lo)

            def solve(c):
                t = slice(c * P, (c + 1) * P)
                pe.wait_ge(row_in, c + 1)
                if c:
                    pe.wait_ge(x_level, LEVELS * c)
                for hd in range(HEADS):
                    last = pe.matmul(mixb[0][:, hd * P:(hd + 1) * P], d_g[:, hd, :], k2c[:, C_TRI:C_TRI + P],
                                     start=True, stop=True)
                last.then_inc(row_done, 1)
                for hd in range(HEADS):
                    o = slice(hd * P, (hd + 1) * P)
                    pe.matmul(mixb[1][:, o], k_t[:, hd, t], k_t[:, hd, t], start=True, stop=True)
                    last = pe.matmul(mixb[2][:, o], q_t[:, hd, t], k_t[:, hd, t], start=True, stop=True)
                last.then_inc(kk_done, 1)
                pe.wait_ge(l_done, c + 1)
                pe.wait_ge(exp_done, 2 * c + 2)
                pe.wait_ge(ld_done, 2 * c + 2)
                for hd in range(HEADS):
                    o = slice(hd * P, (hd + 1) * P)
                    pe.transpose(mixb[0][:, o], d_l[:, hd, :], ident)
                    last = pe.transpose(mixb[1][:, o], d_a[:, hd, :], ident)
                last.then_inc(lt_turned, 1)
                for k in range(1, LEVELS):
                    i = (LEVELS - 1) * c + k
                    pe.wait_ge(m_ready, i)
                    pe.wait_ge(x_level, LEVELS * c + k)
                    for hd in range(HEADS):
                        last = pe.matmul(mixb[2][:, hd * P:(hd + 1) * P], d_m[:, hd, :], d_x[:, hd, :],
                                         start=True, stop=True)
                    last.then_inc(p_done, 1)
                    pe.wait_ge(p_copied, i)
                    for hd in range(HEADS):
                        o = slice(hd * P, (hd + 1) * P)
                        if k < LEVELS - 1:
                            pe.matmul(mixb[0][:, o], y_inv_t[:, c, hd, :], d_p[:, hd, :], start=True, stop=True)
                        last = pe.matmul(mixb[1][:, o], d_p[:, hd, :], y_inv_t[:, c, hd, :], start=True, stop=True)
                    last.then_inc(xp_done, 1)

            def recur(c):
                t = slice(c * P, (c + 1) * P)
                pe.wait_ge(state_done, c + 1)
                pe.wait_ge(x_level, LEVELS * NT)
                for hd in range(HEADS):
                    last = pe.matmul(mixb[0][:, hd * P:(hd + 1) * P], k_t[:, hd, t], state[:, hd, :],
                                     start=True, stop=True)
                last.then_inc(ks_done, 1)
                pe.wait_ge(r_done, c + 1)
                for hd in range(HEADS):
                    last = pe.matmul(mixb[1][:, hd * P:(hd + 1) * P], y_inv_t[:, c, hd, :], u_r[:, hd, :],
                                     start=True, stop=True)
                last.then_inc(vn_done, 1)
                pe.wait_ge(vn_copied, c + 1)
                pe.wait_ge(q_dec, 2 * NT)
                if c:
                    pe.wait_ge(o_copied, c)
                for hd in range(HEADS):
                    o = slice(hd * P, (hd + 1) * P)
                    pe.matmul(mixb[2][:, o], state[:, hd, :], q_t[:, hd, t], start=True, stop=False)
                    pe.matmul(mixb[2][:, o], u_v[:, hd, :], at_t[:, c, hd, :], start=False, stop=True)
                for hd in range(HEADS):
                    last = pe.matmul(mixb[0][:, hd * P:(hd + 1) * P], k_tk[:, c, hd, :], u_v[:, hd, :],
                                     start=True, stop=True)
                last.then_inc(os_done, 1)

            pe.wait_ge(tables_loaded, 32)
            ffn(0)

            n, a = FIRST["pool_in"], OUT0["pool_in"]
            for k in range(KD):
                pe.wait_ge(x_done, KD + k + 1)
                if k == 0:
                    take_block(n)
                    take_bank(a)
                last = product(n % SLOTS, k, acc[a % 4][:, :], x_hi[:, k, :], x_lo[:, k, :], k == 0, k == KD - 1)
            last.then_inc(block_done, 1)
            sum_over_features("norm1", sumsq[:, :], sq_summed, 2 * KD)
            token_sums("token1")
            for j in range(1, 8):
                dense(n + j, a + j, x_hi, x_lo)
            n, a = FIRST["v"], OUT0["v"]
            for half in range(2):
                for t in range(NT):
                    take_bank(a + 4 * half + t)
                for part in range(4):
                    b = n + 4 * half + part
                    take_block(b)
                    for kk in range(2):
                        k = 2 * part + kk
                        w = slice(kk * S, (kk + 1) * S)
                        for t in range(NT):
                            x = slice(t * P, (t + 1) * P)
                            pe.matmul(acc[t][:, :], x_hi[:, k, x], w_hi[:, b % SLOTS, w], start=k == 0, stop=False)
                            pe.matmul(acc[t][:, :], x_lo[:, k, x], w_hi[:, b % SLOTS, w], start=False, stop=False)
                            last = pe.matmul(acc[t][:, :], x_hi[:, k, x], w_lo[:, b % SLOTS, w], start=False,
                                             stop=k == KD - 1)
                    last.then_inc(block_done, 1)
            n, a = FIRST["pool_mix"], OUT0["pool_mix"]
            pe.wait_ge(pooled_done, KD)
            for g in range(4):
                take_block(n + g)
                for m in range(2):
                    take_bank(a + 2 * g + m)
                    for k in range(2):
                        last = product((n + g) % SLOTS, 2 * k + m, acc[(a + 2 * g + m) % 4][:, :],
                                       pooled_hi[:, 2 * g + k, :], pooled_lo[:, 2 * g + k, :], k == 0, k == 1)
                last.then_inc(block_done, 1)
            gated_mix("pool_up", mix_hi, mix_lo, drained, OUT0["pool_mix"] + 8)
            n, a = FIRST["heads"], OUT0["heads"]
            for hd in range(HEADS):
                b, o = n + 6 * hd, a + 6 * hd
                for j in range(2):
                    dense(b + j, o + j, x_hi, x_lo)
                if hd:
                    sum_over_features(f"ret{hd - 1}", sumsq[:, :], ret_sq, hd)
                for j in range(2, 5):
                    dense(b + j, o + j, x_hi, x_lo)
                pe.wait_ge(rotated, 4 * (hd + 1))
                for i in range(NT):
                    if i >= 2:
                        pe.wait_ge(weighted, 4 * hd + i - 1)
                    elif hd:
                        pe.wait_ge(ret_copied, 2 * hd)
                    for d in range(2):
                        last = pe.matmul(mixb[i % 2][:, 0:S - i * P], qk[:, 2 + d, i * P:(i + 1) * P],
                                         qk[:, d, i * P:S], start=d == 0, stop=d == 1)
                    last.then_inc(scores_done, 1)
                dense(b + 5, o + 5, x_hi, x_lo)
                for e in range(2):
                    pe.wait_ge(weighted, 4 * hd + 4)
                    if e == 0 and hd:
                        pe.wait_ge(ret_copied, 2 * hd - 1)
                    bank = mixb[2] if e == 0 else mixb[0]
                    col = hd * DK + e * P
                    for i in range(NT):
                        off = scored_at(i)
                        last = pe.matmul(bank[:, i * P:S], v_tok[:, i, col:col + P], scored[:, off:off + S - i * P],
                                         start=i == 0, stop=i == NT - 1)
                    last.then_inc(av_done, 1)
            gated_mix("ret_up", mix_hi, mix_lo, mix_done, KD)
            n, a = FIRST["mix_out"], OUT0["mix_out"]
            for m in range(KD):
                if m == 0:
                    pe.wait_ge(merged_done, KD)
                dense(n + m, a + m, merged_hi, merged_lo)
            ffn(1)
            ffn(2)

            n, a = FIRST["gdn_qkv"], OUT0["gdn_qkv"]
            pe.wait_ge(x_done, KD * 5)
            sum_over_features("norm4", sumsq[:, :], sq_summed, 5 * KD)
            token_sums("token4")
            pe.wait_ge(wab_split, 1)
            for t in range(NT):
                x = slice(t * P, (t + 1) * P)
                o = mixb[0][:, 8 * t:8 * t + 8]
                for k in range(KD):
                    pe.matmul(o, x_hi[:, k, x], wab_hi[:, k, :], start=k == 0, stop=False)
                    pe.matmul(o, x_lo[:, k, x], wab_hi[:, k, :], start=False, stop=False)
                    last = pe.matmul(o, x_hi[:, k, x], wab_lo[:, k, :], start=False, stop=k == KD - 1)
            last.then_inc(ab_done, 1)
            for j in range(14):
                dense(n + j, a + j, x_hi, x_lo)
                if j >= 2 and (j - 2) % 3 < 2:
                    i = 2 * ((j - 2) // 3) + (j - 2) % 3
                    sum_over_features(f"l2_{i}", square[:, i % 2, :], l2_sq, i + 1)
            pe.wait_ge(g_cum, 1)
            pe.wait_ge(k2_loaded, 16)
            pe.matmul(mixb[0][:, 0:16], k2c[:, C_TRI:C_TRI + P], sm("g"), start=True, stop=True)
            pe.matmul(mixb[0][:, 16:32], ones, sm("g"), start=True, stop=True).then_inc(ab_done, 1)
            for j in range(14, 16):
                dense(n + j, a + j, x_hi, x_lo)
            pe.wait_ge(l2_done, 2 * HEADS)
            pe.wait_ge(conv_act, 3 * HEADS)
            for i in range(2 * HEADS):
                src = k_t if i % 2 == 0 else o_t
                if i >= 2:
                    pe.wait_ge(turned_copied, i - 1)
                for t in range(NT):
                    last = pe.transpose(mixb[1 + i % 2][:, t * P:(t + 1) * P], src[:, i // 2, t * P:(t + 1) * P], ident)
                last.then_inc(turned, 1)
            n, a = FIRST["conv"], OUT0["conv"]
            for j in range(12):
                dense(n + j, a + j, x_hi, x_lo)
                if j >= 5 and j % 3 == 2:
                    i = j // 3 - 1
                    sum_over_features(f"conv{i}", square[:, i % 2, :], c_sq, i + 1, k2c[:, C_GROUP:C_GROUP + P])
            sum_over_features("conv3", square[:, 1, :], c_sq, 4, k2c[:, C_GROUP:C_GROUP + P])
            pe.wait_ge(turned_copied, 2 * HEADS)
            for c in range(NT):
                solve(c)
            for c in range(NT):
                recur(c)
            for i in range(HEADS):
                sum_over_features(f"out{i}", square[:, i % 2, :], o_sq, i + 1)
            n, a = FIRST["mix2_out"], OUT0["mix2_out"]
            for m in range(KD):
                take_block(n + m)
                take_bank(a + m)
                for k in range(KD):
                    if k < 4:
                        pe.wait_ge(c_split, 4)
                        hi, lo = final_hi[:, k, :], final_lo[:, k, :]
                    else:
                        pe.wait_ge(o_split, k - 3)
                        hi, lo = gdn_hi[:, k - 4, :], gdn_lo[:, k - 4, :]
                    last = product((n + m) % SLOTS, k, acc[(a + m) % 4][:, :], hi, lo, k == 0, k == KD - 1)
                last.then_inc(block_done, 1)
            ffn(3)
            sum_over_features("norm6", sumsq[:, :], sq_summed, 7 * KD)


        @block.scalar
        def _(act):
            def split(n):
                if n < NB:
                    slot = n % SLOTS
                    act.wait_ge(loaded[slot], 16 * (n // SLOTS + 1))
                    act.activation(w_hi[:, slot, :], w_raw[:, slot, :], ACT.Copy).then_inc(hi_split, 1)

            def split_in_loop(b, turn):
                slot = b % SLOTS
                act.wait_ge(loaded[slot], 16 * turn + 16 * (b // SLOTS + 1))
                act.activation(w_hi[:, slot, :], w_raw[:, slot, :], ACT.Copy).then_inc(hi_split, 1)

            def residual(r, m):
                gain, phase, _ = NORM[r]
                if phase is None:
                    act.wait_ge(x_loaded[m // 2], 16)
                else:
                    act.wait_ge(drained, OUT0[phase] + m + 1)
                i = KD * r + m
                if i >= 2:
                    act.wait_ge(sq_summed, i - 1)
                act.activation(square[:, m % 2, :], h[:, m, :], ACT.Square).then_inc(sq_done, 1)
                if r == 3:
                    act.wait_ge(chained, m + 1)
                    if m >= 2:
                        act.wait_ge(sq2_summed, m - 1)
                    act.activation(square2[:, m % 2, :], h[:, m, :], ACT.Square).then_inc(sq2_done, 1)
                if gain:
                    act.activation(x_hi[:, m, :], h[:, m, :], ACT.Copy, scale=vcol(gain, m)).then_inc(x_hi_done, 1)

            def take_root(name, out, source, scale, value=None, wait=None):
                n = SUM[name]
                act.wait_ge(summed, n + 1)
                if n:
                    act.wait_ge(inverted, n)
                if wait is not None:
                    act.wait_ge(wait, value)
                act.activation(out, source, ACT.Sqrt, scale=scale, bias=eps).then_inc(rooted, 1)

            def main_root(name):
                take_root(name, root[:, :], sums[:, :], 1.0 / D)

            def ffn(f):
                first, out0 = FIRST[f"ffn{f}_in"], OUT0[f"ffn{f}_in"]

                def half_pair(b, i, turn, u):
                    if isinstance(i, int):
                        split(first + SLOTS * i + b + LEAD)
                    else:
                        split_in_loop(b + LEAD, turn)

                def turn_of(i):
                    q0 = 2 * i
                    turn = i + first // SLOTS
                    for u in range(2):
                        half_pair(2 * u, i, turn, u)
                        act.wait_ge(drained, 2 * q0 + (out0 + 2 * u + 1))
                        act.activation(f_sig[:, u, :], f_gate[:, u, :], ACT.Sigmoid).then_inc(f_sig_done, 1)
                        half_pair(2 * u + 1, i, turn, u)
                        act.wait_ge(drained, 2 * q0 + (out0 + 2 * u + 2))
                        act.activation(hid_hi[:, q0 + u, :], f_hid[:, u, :], ACT.Copy).then_inc(hid_hi_done, 1)

                r = FFN_NORM[f]
                split(first + LEAD)
                main_root(f"norm{r}")
                if f == 2:
                    take_root("norm3b", root[:, :], square2[:, 0, :], 1.0 / D, 1, h_chain)
                for u in range(2):
                    if u:
                        split(first + 2 + LEAD)
                    act.wait_ge(drained, out0 + 2 * u + 1)
                    act.activation(f_sig[:, u, :], f_gate[:, u, :], ACT.Sigmoid).then_inc(f_sig_done, 1)
                    split(first + 2 * u + 1 + LEAD)
                    act.wait_ge(drained, out0 + 2 * u + 2)
                    act.activation(hid_hi[:, u, :], f_hid[:, u, :], ACT.Copy).then_inc(hid_hi_done, 1)
                with act.Fori(1, 2 * KF // SLOTS) as i:
                    turn_of(i)
                first, r = FIRST[f"ffn{f}_out"], [1, 3, 4, 6][f]
                for m in range(KD):
                    for part in range(3):
                        split(first + 3 * m + part + LEAD)
                    residual(r, m)

            def gated_mix(phase, sig0):
                first, out0 = FIRST[phase], OUT0[phase]
                for m in range(KD):
                    split(first + 2 * m + LEAD)
                    if phase == "ret_up" and m == 0:
                        ret_tail_root(HEADS - 1)
                        ret_tail_split(HEADS - 1)
                    act.wait_ge(drained, out0 + 2 * m + 1)
                    branch = 0 if phase == "ret_up" else 1
                    act.activation(m_sig[:, m % 2, :], m_tmp[:, m % 2, :], ACT.Sigmoid,
                                   bias=vcol("gate_bias", KD * branch + m)).then_inc(m_sig_done, 1)
                    split(first + 2 * m + 1 + LEAD)
                    if phase == "ret_up":
                        act.wait_ge(merged_sum, m + 1)
                        act.activation(merged_hi[:, m, :], merged1[:, m, :], ACT.Copy).then_inc(merged_hi_done, 1)

            def ret_tail_root(hd):
                if hd:
                    act.wait_ge(ret_normed, 2 * hd)
                take_root(f"ret{hd}", root[:, :], sums[:, :], 1.0 / DK)

            def ret_tail_split(hd):
                for e in range(2):
                    act.wait_ge(ret_gated, 2 * hd + e + 1)
                    act.activation(mix_hi[:, 2 * hd + e, :], r_raw[:, e, :], ACT.Copy).then_inc(mix_hi_done, 1)

            act.wait_ge(tables_loaded, 32)
            for m in range(KD):
                residual(0, m)
                if m < LEAD:
                    split(m)
            ffn(0)

            n, a = FIRST["pool_in"], OUT0["pool_in"]

            def pooled_split(j):
                act.wait_ge(pool_out_done, j + 1)
                act.activation(pooled_hi[:, j, :], p_out[:, j % 2, :], ACT.Copy).then_inc(pooled_hi_done, 1)

            for j in range(16):
                split(n + j + LEAD)
                if j == 0:
                    main_root("norm1")
                    take_root("token1", rtok[:, 4:8], sums[:, 0:4], 1.0 / D)
                if 3 <= j < 3 + KD:
                    pooled_split(j - 3)
            n, a = FIRST["pool_mix"], OUT0["pool_mix"]
            for g in range(4):
                split(n + g + LEAD)
                act.wait_ge(block_done, n + g + 1)
                for m in range(2):
                    j = 2 * g + m
                    act.activation(mix_hi[:, j, :], acc[(a + j) % 4][:, :], ACT.Copy,
                                   scale=vcol("pool_scale", j)).then_inc(mix_hi_done, 1)
            gated_mix("pool_up", 0)
            n, a = FIRST["heads"], OUT0["heads"]
            for hd in range(HEADS):
                b, o = n + 6 * hd, a + 6 * hd
                split(b + LEAD)
                split(b + 1 + LEAD)
                if hd:
                    ret_tail_root(hd - 1)
                split(b + 2 + LEAD)
                split(b + 3 + LEAD)
                if hd:
                    ret_tail_split(hd - 1)
                for e in range(2):
                    split(b + 4 + e + LEAD)
                    act.wait_ge(drained, o + 4 + e + 1)
                    act.activation(m_sig[:, e, :], m_tmp[:, e, :], ACT.Sigmoid).then_inc(m_sig_done, 1)
                for e in range(2):
                    act.wait_ge(av_done, 2 * hd + e + 1)
                    if hd:
                        act.wait_ge(mix_done, 2 * hd - 1 + e)
                    bank = mixb[2] if e == 0 else mixb[0]
                    act.activation(r_raw[:, e, :], bank[:, :], ACT.Copy)
                    act.activation(square[:, e, :], bank[:, :], ACT.Square).then_inc(ret_copied, 1)
            gated_mix("ret_up", 8)
            n, a = FIRST["mix_out"], OUT0["mix_out"]
            for m in range(KD):
                split(n + m + LEAD)
                residual(2, m)
            ffn(1)
            ffn(2)

            n, a = FIRST["gdn_qkv"], OUT0["gdn_qkv"]
            act.activation(wab_hi[:, :, :], vcol("w_ab", 0, 64).rearrange("p (k n) -> p k n", k=KD),
                           ACT.Copy).then_inc(wab_hi_done, 1)
            main_root("norm4")
            take_root("token4", rtok[:, 4:8], sums[:, 0:4], 1.0 / D)

            def l2_root(i):
                if i:
                    act.wait_ge(l2_done, i)
                take_root(f"l2_{i}", root[:, :], sums[:, :], 1.0)

            step = counter(act, act_step)
            for j in range(16):
                split(n + j + LEAD)
                if 1 <= j <= 12 and (j - 1) % 3 < 2:
                    i, kind = (j - 1) // 3, (j - 1) % 3
                    act.wait_ge(conv_act, j)
                    if 2 * i + kind >= 2:
                        act.wait_ge(rooted, SUM[f"l2_{2 * i + kind - 2}"] + 1)
                    src = (q_t, k_t)[kind]
                    act.activation(square[:, kind, :], src[:, i, :], ACT.Square).then_inc(l2_sq, 1)
                if j < 12:
                    act.wait_ge(conv_done, j + 1)
                    act.activation(c_sig[:, j % 2, :], c_acc[:, j % 2, :], ACT.Sigmoid).then_inc(conv_sig, 1)
                else:
                    act.wait_ge(drained, a + j + 1)
                    act.activation(c_sig[:, j % 2, :], c_acc[:, j % 2, :], ACT.Sigmoid).then_inc(z_sig, 1)
                if j >= 2 and (j - 2) % 3 < 2 and j < 14:
                    l2_root(2 * ((j - 2) // 3) + (j - 2) % 3)
                if j == 3:
                    act.wait_ge(ab_ready, 1)
                    act.activation(sm("beta"), sm("beta"), ACT.Sigmoid)
                    act.activation(sm("neg_a")[:, 0:4], vcol("A_log", 0, 4), ACT.Exp)
                    step(act.activation(sm("u"), sm("nz"), ACT.Exp))
                    act.activation(sm("w"), sm("u"), ACT.Copy, bias=1.0)
                    act.activation(sm("lnw"), sm("u"), ACT.Ln, bias=one).then_inc(ab_act, 1)
            act.wait_ge(ab_done, 2)
            act.activation(sm("cum"), mixb[0][:, 0:16], ACT.Copy)
            act.activation(sm("total"), mixb[0][:, 16:32], ACT.Copy)
            act.activation(sm("e_cum"), mixb[0][:, 0:16], ACT.Exp)
            act.activation(sm("e_total"), mixb[0][:, 16:32], ACT.Exp).then_inc(ab_act, 1)
            act.wait_ge(ab_ready, 2)
            act.activation(sm("e_left"), sm("e_left"), ACT.Exp).then_inc(ab_act, 1)
            for i in range(2 * HEADS):
                act.wait_ge(turned, i + 1)
                dst = k_tk if i % 2 == 0 else v_tk
                act.activation(dst[:, :, i // 2, :], mixb[1 + i % 2][:, :].rearrange("p (c n) -> p c n", c=NT),
                               ACT.Copy).then_inc(turned_copied, 1)
            n, a = FIRST["conv"], OUT0["conv"]

            def conv_root(i):
                if i:
                    act.wait_ge(c_normed, i)
                take_root(f"conv{i}", root[:, :], sums[:, :], 1.0 / 64)

            def conv_split(i):
                act.wait_ge(c_normed, i + 1)
                act.activation(final_hi[:, i, :], c_y[:, i % 2, :], ACT.Copy).then_inc(c_hi, 1)

            for j in range(12):
                split(n + j + LEAD)
                if j % 3 == 0 and j:
                    i = j // 3 - 1
                    act.wait_ge(c_prod, i + 1)
                    if i >= 2:
                        act.wait_ge(rooted, SUM[f"conv{i - 2}"] + 1)
                    act.activation(square[:, i % 2, :], c_y[:, i % 2, :], ACT.Square).then_inc(c_sq, 1)
                if j % 3 == 2 and j >= 5:
                    conv_root(j // 3 - 1)
                    conv_split(j // 3 - 1)
            act.wait_ge(c_prod, 4)
            act.wait_ge(rooted, SUM["conv1"] + 1)
            act.activation(square[:, 1, :], c_y[:, 1, :], ACT.Square).then_inc(c_sq, 1)
            conv_root(3)
            conv_split(3)

            def solve(c):
                act.wait_ge(diff_done, c + 1)
                act.activation(d_exp[:, :, :], d_exp[:, :, :], ACT.Exp).then_inc(exp_done, 1)
                act.activation(d_row[:, :, :], bank_h(mixb[0]), ACT.Exp).then_inc(exp_done, 1)
                act.wait_ge(lt_turned, c + 1)
                act.activation(d_lt[:, :, :], bank_h(mixb[0]), ACT.Copy)
                act.activation(at_t[:, c, :, :], bank_h(mixb[1]), ACT.Copy).then_inc(lt_copied, 1)
                for k in range(1, LEVELS):
                    act.wait_ge(p_done, (LEVELS - 1) * c + k)
                    act.activation(d_p[:, :, :], bank_h(mixb[2]), ACT.Copy).then_inc(p_copied, 1)

            for c in range(NT):
                solve(c)
            for c in range(NT):
                act.wait_ge(vn_done, c + 1)
                act.activation(u_v[:, :, :], bank_h(mixb[1]), ACT.Copy).then_inc(vn_copied, 1)
                act.wait_ge(os_done, c + 1)
                act.activation(o_t[:, :, c * P:(c + 1) * P], bank_h(mixb[2]), ACT.Copy).then_inc(o_copied, 1)
            act.wait_ge(o_copied, NT)
            for i in range(2):
                act.activation(square[:, i, :], o_t[:, i, :], ACT.Square).then_inc(o_sq, 1)
            for i in range(HEADS):
                if i:
                    act.wait_ge(o_normed, i)
                take_root(f"out{i}", root[:, :], sums[:, :], 1.0 / W2)
                if i + 2 < HEADS:
                    act.activation(square[:, i % 2, :], o_t[:, i + 2, :], ACT.Square).then_inc(o_sq, 1)
                act.wait_ge(o_gated, i + 1)
                act.activation(gdn_hi[:, i, :], o_t[:, i, :], ACT.Copy).then_inc(o_hi, 1)
            n, a = FIRST["mix2_out"], OUT0["mix2_out"]
            for m in range(KD):
                split(n + m + LEAD)
                residual(5, m)
            ffn(3)
            main_root("norm6")

        @block.vector
        def _(dve):
            step = counter(dve, dve_step)

            def split(n):
                if n < NB:
                    slot = n % SLOTS
                    dve.wait_ge(hi_split, n + 1)
                    dve.tensor_tensor(w_lo[:, slot, :], w_raw[:, slot, :], w_hi[:, slot, :].bitcast(F32),
                                      ALU.subtract).then_inc(lo_split, 1)

            def residual(r, m):
                gain, phase, scale = NORM[r]
                if phase:
                    a = OUT0[phase] + m
                    first = FIRST[phase]
                    dve.wait_ge(block_done, first + (3 * m + 3 if phase.startswith("ffn") else m + 1))
                    if r == 4 and m == 0:
                        dve.wait_ge(h_final, KD)
                    dve.scalar_tensor_tensor(h[:, m, :], acc[a % 4][:, :], scale, h[:, m, :], ALU.mult,
                                             ALU.add).then_inc(drained, 1)
                if r == 3:
                    dve.wait_ge(sq_done, KD * r + m + 1)
                    dve.tensor_scalar(h[:, m, :], h[:, m, :], vcol("norm_final", m), None,
                                      ALU.mult).then_inc(chained, 1)
                if gain:
                    dve.wait_ge(x_hi_done, KD * [0, 1, 2, 3, 4, 5][r] + m + 1)
                    dve.scalar_tensor_tensor(x_lo[:, m, :], h[:, m, :], vcol(gain, m), x_hi[:, m, :].bitcast(F32),
                                             ALU.mult, ALU.subtract).then_inc(x_done, 1)

            def invert(name, out, source):
                dve.wait_ge(rooted, SUM[name] + 1)
                dve.reciprocal(out, source).then_inc(inverted, 1)
                dve.wait_ge(inverted, SUM[name] + 1)

            def ffn(f):
                first, out0 = FIRST[f"ffn{f}_in"], OUT0[f"ffn{f}_in"]
                r = FFN_NORM[f]
                split(first + LEAD)
                invert(f"norm{r}", rstd[:, :], root[:, :])
                if f == 2:
                    step(dve.tensor_copy(r_one[:, :], rstd[:, :]))
                    step(dve.tensor_tensor(square2[:, 0, :], rstd[:, :], rstd[:, :], ALU.mult))
                    dve.wait_ge(summed, SUM["norm3b"] + 1)
                    dve.tensor_tensor(square2[:, 0, :], sums[:, :], square2[:, 0, :], ALU.mult).then_inc(h_chain, 1)
                    invert("norm3b", root[:, :], root[:, :])
                    step(dve.tensor_tensor(rstd[:, :], r_one[:, :], root[:, :], ALU.mult))
                for u in range(2):
                    if u:
                        split(first + 2 * u + LEAD)
                    dve.wait_ge(block_done, first + 2 * u + 1)
                    dve.tensor_tensor(f_gate[:, u, :], acc[2 * u][:, :], rstd[:, :], ALU.mult).then_inc(drained, 1)
                    split(first + 2 * u + 1 + LEAD)
                    dve.wait_ge(block_done, first + 2 * u + 2)
                    dve.wait_ge(f_mul_done, KF * f + u + 1)
                    dve.tensor_tensor(f_hid[:, u, :], acc[2 * u + 1][:, :], f_mul[:, u, :],
                                      ALU.mult).then_inc(drained, 1)
                with dve.Fori(1, 2 * KF // SLOTS) as i:
                    for u in range(2):
                        for b in (2 * u, 2 * u + 1):
                            slot = (b + LEAD) % SLOTS
                            dve.wait_ge(hi_split, SLOTS * i + (first + b + LEAD + 1))
                            dve.tensor_tensor(w_lo[:, slot, :], w_raw[:, slot, :], w_hi[:, slot, :].bitcast(F32),
                                              ALU.subtract).then_inc(lo_split, 1)
                            dve.wait_ge(block_done, SLOTS * i + (first + b + 1))
                            if b % 2 == 0:
                                dve.tensor_tensor(f_gate[:, u, :], acc[b][:, :], rstd[:, :],
                                                  ALU.mult).then_inc(drained, 1)
                            else:
                                dve.wait_ge(f_mul_done, 2 * i + (KF * f + u + 1))
                                dve.tensor_tensor(f_hid[:, u, :], acc[b][:, :], f_mul[:, u, :],
                                                  ALU.mult).then_inc(drained, 1)
                first, r = FIRST[f"ffn{f}_out"], [1, 3, 4, 6][f]
                for m in range(KD):
                    for part in range(3):
                        split(first + 3 * m + part + LEAD)
                    residual(r, m)

            def gated_mix(phase, sig0):
                first, out0 = FIRST[phase], OUT0[phase]
                for m in range(KD):
                    split(first + 2 * m + LEAD)
                    if phase == "ret_up" and m == 0:
                        ret_tail_norm(HEADS - 1)
                        ret_tail_split(HEADS - 1)
                    dve.wait_ge(block_done, first + 2 * m + 1)
                    if sig0 + m >= 2:
                        dve.wait_ge(m_sig_done, sig0 + m - 1)
                    if phase == "ret_up" and m < 2:
                        dve.wait_ge(g_ready, 2 * HEADS)
                    dve.tensor_tensor(m_tmp[:, m % 2, :], acc[(out0 + 2 * m) % 4][:, :], rstd[:, :],
                                      ALU.mult).then_inc(drained, 1)
                    split(first + 2 * m + 1 + LEAD)
                    dve.wait_ge(block_done, first + 2 * m + 2)
                    dve.wait_ge(m_sig_done, sig0 + m + 1)
                    bank = acc[(out0 + 2 * m + 1) % 4][:, :]
                    if phase == "pool_up":
                        dve.tensor_tensor(merged1[:, m, :], bank, m_sig[:, m % 2, :], ALU.mult).then_inc(drained, 1)
                    else:
                        dve.tensor_tensor(m_tmp[:, m % 2, :], bank, m_sig[:, m % 2, :], ALU.mult).then_inc(drained, 1)
                        dve.wait_ge(drained, out0 + 2 * m + 2)
                        dve.tensor_tensor(merged1[:, m, :], merged1[:, m, :], m_tmp[:, m % 2, :],
                                          ALU.add).then_inc(merged_sum, 1)
                        dve.wait_ge(merged_hi_done, m + 1)
                        dve.tensor_tensor(merged_lo[:, m, :], merged1[:, m, :], merged_hi[:, m, :].bitcast(F32),
                                          ALU.subtract).then_inc(merged_done, 1)

            def ret_tail_norm(hd):
                invert(f"ret{hd}", root[:, :], root[:, :])
                for e in range(2):
                    dve.tensor_tensor(r_raw[:, e, :], r_raw[:, e, :], root[:, :], ALU.mult).then_inc(ret_normed, 1)

            def ret_tail_split(hd):
                for e in range(2):
                    j = 2 * hd + e
                    dve.wait_ge(mix_hi_done, KD + j + 1)
                    dve.tensor_tensor(mix_lo[:, j, :], r_raw[:, e, :], mix_hi[:, j, :].bitcast(F32),
                                      ALU.subtract).then_inc(mix_done, 1)

            dve.wait_ge(tables_loaded, 32)
            for m in range(KD):
                residual(0, m)
                if m < LEAD:
                    split(m)
            ffn(0)

            n, a = FIRST["pool_in"], OUT0["pool_in"]

            def pooled_split(j):
                dve.wait_ge(pooled_hi_done, j + 1)
                dve.tensor_tensor(pooled_lo[:, j, :], p_out[:, j % 2, :], pooled_hi[:, j, :].bitcast(F32),
                                  ALU.subtract).then_inc(pooled_done, 1)

            for j in range(8):
                split(n + j + LEAD)
                if j == 0:
                    invert("norm1", rstd[:, :], root[:, :])
                    invert("token1", rtok[:, 0:4], rtok[:, 4:8])
                    dve.wait_ge(zeroed, 1)
                dve.wait_ge(block_done, n + j + 1)
                if j >= 2:
                    dve.wait_ge(pool_out_done, j - 1)
                dve.tensor_tensor(p_raw[:, j % 2, PADP:], acc[(a + j) % 4][:, :], rstd[:, :],
                                  ALU.mult).then_inc(drained, 1)
                if j >= 3:
                    pooled_split(j - 3)
            n, a = FIRST["v"], OUT0["v"]
            for half in range(2):
                for part in range(4):
                    j = 4 * half + part
                    split(n + j + LEAD)
                    if j < 3:
                        pooled_split(5 + j)
                dve.wait_ge(block_done, n + 4 * half + 4)
                for t in range(NT):
                    dve.tensor_scalar(v_tok[:, t, half * S:(half + 1) * S], acc[t][:, :], rtok[:, t:t + 1], None,
                                      ALU.mult).then_inc(drained, 1)
            n, a = FIRST["pool_mix"], OUT0["pool_mix"]
            for g in range(4):
                split(n + g + LEAD)
                for m in range(2):
                    j = 2 * g + m
                    dve.wait_ge(mix_hi_done, j + 1)
                    dve.scalar_tensor_tensor(mix_lo[:, j, :], acc[(a + j) % 4][:, :], vcol("pool_scale", j),
                                             mix_hi[:, j, :].bitcast(F32), ALU.mult, ALU.subtract).then_inc(drained, 1)
            gated_mix("pool_up", 0)
            n, a = FIRST["heads"], OUT0["heads"]
            dve.wait_ge(k1_loaded, 16)
            cos, sin = k1c[:, C_COS:C_COS + S], k1c[:, C_SIN:C_SIN + S]
            step(dve.tensor_tensor(cos, cos, rstd[:, :], ALU.mult))
            step(dve.tensor_tensor(sin, sin, rstd[:, :], ALU.mult))
            for hd in range(HEADS):
                b, o = n + 6 * hd, a + 6 * hd

                def rotate(pair):
                    w = 2 * hd + pair
                    split(b + 2 * pair + LEAD)
                    split(b + 2 * pair + 1 + LEAD)
                    dve.wait_ge(block_done, b + 2 * pair + 2)
                    first, second = (acc[(o + 2 * pair + i) % 4][:, :] for i in range(2))
                    if w:
                        dve.wait_ge(rotated, 2 * w)
                    dve.tensor_tensor(rot[:, 0, :], first, cos, ALU.mult)
                    dve.tensor_tensor(rot[:, 1, :], second, sin, ALU.mult)
                    dve.tensor_tensor(rot[:, 2, :], first, sin, ALU.mult).then_inc(drained, 1)
                    dve.tensor_tensor(rot[:, 3, :], second, cos, ALU.mult).then_inc(drained, 1)

                rotate(0)
                if hd:
                    ret_tail_norm(hd - 1)
                rotate(1)
                if hd:
                    ret_tail_split(hd - 1)
                for e in range(2):
                    split(b + 4 + e + LEAD)
                    dve.wait_ge(block_done, b + 4 + e + 1)
                    if hd:
                        dve.wait_ge(g_ready, 2 * hd - 1 + e)
                    else:
                        dve.wait_ge(m_sig_done, 8)
                    dve.tensor_tensor(m_tmp[:, e, :], acc[(o + 4 + e) % 4][:, :], rstd[:, :],
                                      ALU.mult).then_inc(drained, 1)
                    if e == 0:
                        if hd:
                            dve.wait_ge(av_done, 2 * hd)
                        for i in range(NT):
                            dve.wait_ge(scores_done, 4 * hd + i + 1)
                            off, width = scored_at(i), S - i * P
                            dve.tensor_tensor(scored[:, off:off + width], mixb[i % 2][:, 0:width],
                                              k1c[:, C_DECAY + hd * S:C_DECAY + hd * S + width],
                                              ALU.mult).then_inc(weighted, 1)
            gated_mix("ret_up", 16)
            n, a = FIRST["mix_out"], OUT0["mix_out"]
            for m in range(KD):
                split(n + m + LEAD)
                residual(2, m)
            ffn(1)
            ffn(2)

            n, a = FIRST["gdn_qkv"], OUT0["gdn_qkv"]
            dve.wait_ge(wab_hi_done, 1)
            dve.tensor_tensor(wab_lo[:, :, :], vcol("w_ab", 0, 64).rearrange("p (k n) -> p k n", k=KD),
                              wab_hi[:, :, :].bitcast(F32), ALU.subtract).then_inc(wab_split, 1)
            invert("norm4", rstd[:, :], root[:, :])
            invert("token4", rtok[:, 0:4], rtok[:, 4:8])
            dve.wait_ge(zeroed, 2)
            dve.wait_ge(ab_done, 1)
            ab = mixb[0][:, 0:32].rearrange("p (c n) -> p c n", c=NT)
            token = rtok[:, 0:4].unsqueeze(2).to_broadcast([P, NT, HEADS])

            def ch(name):
                return sm(name).rearrange("p (c n) -> p c n", c=NT)

            dve.tensor_tensor(ch("beta"), ab[:, :, 0:4], token, ALU.mult)
            step(dve.tensor_tensor(ch("z"), ab[:, :, 4:8], token, ALU.mult))
            step(dve.tensor_tensor(ch("z"), ch("z"),
                                   vcol("dt_bias", 0, 4).unsqueeze(1).to_broadcast([P, NT, HEADS]), ALU.add))
            dve.scalar_tensor_tensor(sm("nz"), sm("z"), -1.0, sm("z"), ALU.mult, ALU.min).then_inc(ab_ready, 1)

            def log_decay():
                dve.wait_ge(ab_act, 1)
                step(dve.tensor_scalar(sm("d"), sm("w"), -1.0, None, ALU.add))
                step(dve.tensor_scalar(sm("eq"), sm("d"), 0.0, None, ALU.is_equal))
                dve.tensor_tensor(sm("d"), sm("d"), sm("eq"), ALU.add)
                step(dve.tensor_tensor(sm("lnw"), sm("lnw"), sm("eq"), ALU.add))
                step(dve.reciprocal(sm("d"), sm("d")))
                step(dve.tensor_tensor(sm("lnw"), sm("lnw"), sm("d"), ALU.mult))
                step(dve.tensor_tensor(sm("lnw"), sm("lnw"), sm("u"), ALU.mult))
                step(dve.scalar_tensor_tensor(sm("lnw"), sm("z"), 0.0, sm("lnw"), ALU.max, ALU.add))
                step(dve.tensor_scalar(sm("lnw"), sm("lnw"), -1.0, None, ALU.mult))
                dve.tensor_tensor(ch("g"), ch("lnw"),
                                  sm("neg_a")[:, 0:4].unsqueeze(1).to_broadcast([P, NT, HEADS]),
                                  ALU.mult).then_inc(g_cum, 1)

            def l2_norm(i):
                hd, kind = i // 2, i % 2
                invert(f"l2_{i}", root[:, :], root[:, :])
                dst = (q_t, k_t)[kind][:, hd, :]
                dve.scalar_tensor_tensor(dst, dst, W2 ** -0.5 if kind == 0 else 1.0, root[:, :], ALU.mult,
                                         ALU.mult).then_inc(l2_done, 1)

            for j in range(16):
                split(n + j + LEAD)
                dve.wait_ge(block_done, n + j + 1)
                bank = acc[(a + j) % 4][:, :]
                if j < 12:
                    if j >= 2:
                        dve.wait_ge(conv_act, j - 1)
                    u = j % 2
                    dve.tensor_tensor(c_raw[:, u, 4:], bank, rstd[:, :], ALU.mult).then_inc(drained, 1)
                    dve.wait_ge(drained, a + j + 1)
                    channel = 4 * (j % 3) + j // 3
                    for tap in range(4):
                        w = vcol("gdn_conv_w_2", 12 * tap + channel)
                        src = c_raw[:, u, 1 + tap:1 + tap + S]
                        if tap == 0:
                            step(dve.tensor_scalar(c_acc[:, u, :], src, w, None, ALU.mult))
                        else:
                            ins = dve.scalar_tensor_tensor(c_acc[:, u, :], src, w, c_acc[:, u, :], ALU.mult, ALU.add)
                            if tap == 3:
                                ins.then_inc(conv_done, 1)
                            else:
                                step(ins)
                else:
                    if j < 14:
                        dve.wait_ge(conv_act, j - 1)
                    else:
                        dve.wait_ge(z_ready, j - 13)
                    dve.tensor_tensor(c_acc[:, j % 2, :], bank, rstd[:, :], ALU.mult).then_inc(drained, 1)
                if j >= 2 and (j - 2) % 3 < 2 and j < 14:
                    l2_norm(2 * ((j - 2) // 3) + (j - 2) % 3)
                if j == 4:
                    log_decay()
            dve.wait_ge(k2_loaded, 16)
            dve.wait_ge(ab_act, 2)
            dve.tensor_tensor(sm("e_left"), sm("total"), sm("cum"), ALU.subtract).then_inc(ab_ready, 1)
            n, a = FIRST["conv"], OUT0["conv"]

            def conv_norm(i):
                invert(f"conv{i}", root[:, :], root[:, :])
                dve.scalar_tensor_tensor(c_y[:, i % 2, :], c_y[:, i % 2, :], vcol("conv_out_norm_2", i), root[:, :],
                                         ALU.mult, ALU.mult).then_inc(c_normed, 1)
                dve.wait_ge(c_hi, i + 1)
                dve.tensor_tensor(final_lo[:, i, :], c_y[:, i % 2, :], final_hi[:, i, :].bitcast(F32),
                                  ALU.subtract).then_inc(c_split, 1)

            dve.wait_ge(z_ready, HEADS)
            for j in range(12):
                i, u = j // 3, (j // 3) % 2
                split(n + j + LEAD)
                dve.wait_ge(block_done, n + j + 1)
                bank = acc[(a + j) % 4][:, :]
                if j % 3 == 0:
                    dve.tensor_tensor(c_gate[:, u, :], bank, rstd[:, :], ALU.mult).then_inc(drained, 1)
                elif j % 3 == 1:
                    dve.tensor_tensor(c_sig[:, u, :], bank, rstd[:, :], ALU.mult).then_inc(drained, 1)
                    dve.wait_ge(c_gated, i + 1)
                    for tap in range(3):
                        w = vcol("conv_short_w_2", 4 * tap + i)
                        src = c_raw[:, u, 2 + tap:2 + tap + S]
                        if tap == 0:
                            step(dve.tensor_scalar(c_acc[:, u, :], src, w, None, ALU.mult))
                        else:
                            ins = dve.scalar_tensor_tensor(c_acc[:, u, :], src, w, c_acc[:, u, :], ALU.mult, ALU.add)
                            if tap == 1:
                                step(ins)
                            else:
                                ins.then_inc(c_conv, 1)
                else:
                    dve.tensor_tensor(c_gate[:, u, :], bank, rstd[:, :], ALU.mult).then_inc(drained, 1)
                    if j >= 5:
                        conv_norm(i - 1)
            conv_norm(3)

            def solve(c):
                dve.wait_ge(row_done, c + 1)
                step(dve.tensor_tensor(d_exp[:, :, :], per_head("cum", c), bank_h(mixb[0]), ALU.subtract))
                dve.scalar_tensor_tensor(d_exp[:, :, :], d_exp[:, :, :], 0.0, over_heads(C_STRICT), ALU.min,
                                         ALU.mult).then_inc(diff_done, 1)
                dve.wait_ge(decay_ready, c + 1)
                dve.wait_ge(kk_done, c + 1)
                dve.tensor_tensor(d_l[:, :, :], bank_h(mixb[1]), d_exp[:, :, :], ALU.mult).then_inc(ld_done, 1)
                dve.tensor_tensor(d_a[:, :, :], bank_h(mixb[2]), d_exp[:, :, :], ALU.mult).then_inc(ld_done, 1)
                dve.wait_ge(l_done, c + 1)
                step(dve.tensor_tensor(d_t[:, :, :], d_l[:, :, :], over_heads(C_LEVEL), ALU.mult))
                step(dve.tensor_tensor(d_x[:, :, :], ident_h, d_t[:, :, :], ALU.subtract))
                dve.wait_ge(lt_copied, c + 1)
                step(dve.tensor_tensor(d_t[:, :, :], d_lt[:, :, :], over_heads(C_LEVEL + P), ALU.mult))
                dve.tensor_tensor(y_inv_t[:, c, :, :], ident_h, d_t[:, :, :], ALU.subtract).then_inc(x_level, 1)
                for k in range(1, LEVELS):
                    dve.wait_ge(xp_done, (LEVELS - 1) * c + k)
                    if k < LEVELS - 1:
                        dve.tensor_tensor(d_x[:, :, :], d_x[:, :, :], bank_h(mixb[0]), ALU.subtract)
                    dve.tensor_tensor(y_inv_t[:, c, :, :], y_inv_t[:, c, :, :], bank_h(mixb[1]),
                                      ALU.subtract).then_inc(x_level, 1)

            for c in range(NT):
                solve(c)
            dve.wait_ge(x_level, LEVELS * NT)
            dve.memset(state[:, :, :], 0.0).then_inc(state_done, 1)
            for c in range(NT):
                dve.wait_ge(ks_done, c + 1)
                step(dve.tensor_tensor(u_t[:, :, :], bank_h(mixb[0]), per_head("e_cum", c), ALU.mult))
                step(dve.tensor_tensor(u_t[:, :, :], v_tk[:, c, :, :], u_t[:, :, :], ALU.subtract))
                dve.tensor_tensor(u_r[:, :, :], u_t[:, :, :], per_head("beta", c), ALU.mult).then_inc(r_done, 1)
                dve.wait_ge(os_done, c + 1)
                step(dve.tensor_tensor(u_state[:, :, :], state[:, :, :], per_head("e_total", c), ALU.mult))
                dve.tensor_tensor(state[:, :, :], u_state[:, :, :], bank_h(mixb[0]), ALU.add).then_inc(state_done, 1)
            for i in range(HEADS):
                invert(f"out{i}", root[:, :], root[:, :])
                dve.scalar_tensor_tensor(o_t[:, i, :], o_t[:, i, :], vcol("gdn_out_norm_2", 0), root[:, :], ALU.mult,
                                         ALU.mult).then_inc(o_normed, 1)
                dve.wait_ge(o_hi, i + 1)
                dve.tensor_tensor(gdn_lo[:, i, :], o_t[:, i, :], gdn_hi[:, i, :].bitcast(F32),
                                  ALU.subtract).then_inc(o_split, 1)
            n, a = FIRST["mix2_out"], OUT0["mix2_out"]
            for m in range(KD):
                split(n + m + LEAD)
                residual(5, m)
            ffn(3)
            invert("norm6", rstd[:, :], root[:, :])
            for m in range(KD):
                dve.scalar_tensor_tensor(h[:, m, :], h[:, m, :], vcol("final_norm_2", m), rstd[:, :], ALU.mult,
                                         ALU.mult).then_inc(y_ready, 1)

        @block.gpsimd
        def _(pool):
            step = counter(pool, pool_step)

            def add_square(r, m):
                i = KD * r + m
                pool.wait_ge(sq_done, i + 1)
                if m == 0:
                    if r:
                        pool.wait_ge(summed, SUM[f"norm{r}"])
                    pool.tensor_copy(sumsq[:, :], square[:, 0, :]).then_inc(sq_summed, 1)
                else:
                    pool.wait_ge(sq_summed, i)
                    pool.tensor_tensor(sumsq[:, :], sumsq[:, :], square[:, m % 2, :], ALU.add).then_inc(sq_summed, 1)
                if r == 3:
                    pool.wait_ge(sq2_done, m + 1)
                    if m == 0:
                        pool.tensor_copy(sumsq2[:, :], square2[:, 0, :]).then_inc(sq2_summed, 1)
                    else:
                        pool.wait_ge(sq2_summed, m)
                        pool.tensor_tensor(sumsq2[:, :], sumsq2[:, :], square2[:, m % 2, :],
                                           ALU.add).then_inc(sq2_summed, 1)

            def ffn(f):
                out0 = OUT0[f"ffn{f}_in"]
                with pool.Fori(0, KF // 2) as i:
                    for u in range(2):
                        q = 2 * i + (KF * f + u)
                        pool.wait_ge(f_sig_done, q + 1)
                        pool.tensor_tensor(f_mul[:, u, :], f_gate[:, u, :], f_sig[:, u, :], ALU.mult).then_inc(f_step, 1)
                        pool.wait_ge(f_step, q + 1)
                        pool.tensor_tensor(f_mul[:, u, :], f_mul[:, u, :], rstd[:, :], ALU.mult).then_inc(f_mul_done, 1)
                        pool.wait_ge(hid_hi_done, q + 1)
                        pool.tensor_tensor(hid_lo[:, 2 * i + u, :], f_hid[:, u, :], hid_hi[:, 2 * i + u, :].bitcast(F32),
                                           ALU.subtract).then_inc(hid_done, 1)
                if f == 2:
                    for m in range(KD):
                        pool.tensor_tensor(h[:, m, :], h[:, m, :], r_one[:, :], ALU.mult).then_inc(h_final, 1)
                r = [1, 3, 4, 6][f]
                for m in range(KD):
                    add_square(r, m)

            for m in range(KD):
                add_square(0, m)
            ffn(0)

            pool.memset(p_raw[:, :, 0:PADP], 0.0)
            pool.memset(p_sum[:, :, 0:PADP], 0.0).then_inc(zeroed, 1)
            pool.wait_ge(summed, SUM["token1"] + 1)
            pool.dma_start(k1c[:, :], const1).then_inc(k1_loaded, 16)
            pool.wait_ge(zeroed, 1)
            for j in range(8):
                g, u = j // 2, j % 2
                pool.wait_ge(drained, OUT0["pool_in"] + j + 1)
                src, width, to = p_raw[:, u, :], 1, 0
                while width < POOL[g]:
                    step(pool.tensor_tensor(p_sum[:, to, PADP:], src[:, PADP:], src[:, PADP - width:PADP + S - width],
                                            ALU.add))
                    src, width, to = p_sum[:, to, :], 2 * width, 1 - to
                if j >= 2:
                    pool.wait_ge(pooled_done, j - 1)
                step(pool.tensor_scalar(p_out[:, u, :], src[:, PADP:], 1.0 / POOL[g], None, ALU.mult))
                step(pool.tensor_tensor(p_out[:, u, 0:PADP], src[:, PADP:2 * PADP],
                                        cst[:, C_EDGE + g * PADP:C_EDGE + (g + 1) * PADP], ALU.mult))
                pool.tensor_tensor(p_out[:, u, :], p_out[:, u, :], p_raw[:, u, PADP:],
                                   ALU.subtract).then_inc(pool_out_done, 1)
            a = OUT0["heads"]

            def ret_gate(hd):
                for e in range(2):
                    pool.wait_ge(ret_normed, 2 * hd + e + 1)
                    pool.tensor_tensor(r_raw[:, e, :], r_raw[:, e, :], silu_g[:, e, :], ALU.mult).then_inc(ret_gated, 1)

            for hd in range(HEADS):
                o = a + 6 * hd
                for pair in range(2):
                    pool.wait_ge(drained, o + 2 * pair + 1)
                    pool.tensor_tensor(qk[:, 2 * pair, :], rot[:, 0, :], rot[:, 1, :], ALU.subtract).then_inc(rotated, 1)
                    pool.wait_ge(drained, o + 2 * pair + 2)
                    pool.tensor_tensor(qk[:, 2 * pair + 1, :], rot[:, 2, :], rot[:, 3, :], ALU.add).then_inc(rotated, 1)
                    if pair == 0 and hd:
                        ret_gate(hd - 1)
                for e in range(2):
                    pool.wait_ge(m_sig_done, 8 + 2 * hd + e + 1)
                    pool.tensor_tensor(silu_g[:, e, :], m_tmp[:, e, :], m_sig[:, e, :], ALU.mult).then_inc(g_ready, 1)
                pool.wait_ge(ret_copied, 2 * hd + 2)
                pool.wait_ge(summed, SUM[f"ret{hd}"])
                pool.tensor_tensor(sumsq[:, :], square[:, 0, :], square[:, 1, :], ALU.add).then_inc(ret_sq, 1)
            ret_gate(HEADS - 1)
            for m in range(KD):
                add_square(2, m)
            ffn(1)
            ffn(2)

            pool.memset(c_raw[:, :, 0:4], 0.0).then_inc(zeroed, 1)
            pool.wait_ge(summed, SUM["token4"] + 1)
            pool.dma_start(k2c[:, :], const2).then_inc(k2_loaded, 16)
            for j in range(16):
                if j < 12:
                    pool.wait_ge(conv_sig, j + 1)
                    dst = (q_t, k_t, o_t)[j % 3][:, j // 3, :]
                    pool.tensor_tensor(dst, c_acc[:, j % 2, :], c_sig[:, j % 2, :], ALU.mult).then_inc(conv_act, 1)
                else:
                    pool.wait_ge(z_sig, j - 11)
                    pool.tensor_tensor(z_t[:, j - 12, :], c_acc[:, j % 2, :], c_sig[:, j % 2, :],
                                       ALU.mult).then_inc(z_ready, 1)
            for i in range(4):
                u = i % 2
                pool.wait_ge(drained, OUT0["conv"] + 3 * i + 2)
                pool.tensor_tensor(c_raw[:, u, 4:], c_sig[:, u, :], c_gate[:, u, :], ALU.mult).then_inc(c_gated, 1)
                pool.wait_ge(drained, OUT0["conv"] + 3 * i + 3)
                pool.wait_ge(c_conv, i + 1)
                if i >= 2:
                    pool.wait_ge(c_split, i - 1)
                pool.tensor_tensor(c_y[:, u, :], c_acc[:, u, :], c_gate[:, u, :], ALU.mult).then_inc(c_prod, 1)
            pool.wait_ge(k2_loaded, 16)
            pool.wait_ge(c_split, 4)
            pool.wait_ge(ab_act, 3)
            pool.wait_ge(turned_copied, 2 * HEADS)

            def solve(c):
                pool.tensor_copy(d_g[:, :, :], per_head("g", c)).then_inc(row_in, 1)
                pool.wait_ge(exp_done, 2 * c + 1)
                pool.tensor_tensor(d_exp[:, :, :], d_exp[:, :, :], over_heads(C_CAUSAL), ALU.mult).then_inc(decay_ready, 1)
                pool.wait_ge(ld_done, 2 * c + 1)
                pool.tensor_tensor(d_l[:, :, :], d_l[:, :, :], per_head("beta", c), ALU.mult).then_inc(l_done, 1)
                t = slice(c * P, (c + 1) * P)
                pool.wait_ge(exp_done, 2 * c + 2)
                pool.wait_ge(ld_done, 2 * c + 2)
                pool.tensor_tensor(q_t[:, :, t], q_t[:, :, t], d_row[:, :, :], ALU.mult).then_inc(q_dec, 1)
                pool.tensor_tensor(k_tk[:, c, :, :], k_tk[:, c, :, :], per_head("e_left", c), ALU.mult).then_inc(q_dec, 1)
                pool.wait_ge(lt_copied, c + 1)
                for k in range(1, LEVELS):
                    i = (LEVELS - 1) * c + k
                    if i >= 2:
                        pool.wait_ge(p_done, i - 1)
                    pool.tensor_tensor(d_m[:, :, :], d_lt[:, :, :], over_heads(C_LEVEL + (k + 1) * P),
                                       ALU.mult).then_inc(m_ready, 1)

            for c in range(NT):
                solve(c)
            for i in range(HEADS):
                pool.wait_ge(o_normed, i + 1)
                pool.tensor_tensor(o_t[:, i, :], o_t[:, i, :], z_t[:, i, :], ALU.mult).then_inc(o_gated, 1)
            for m in range(KD):
                add_square(5, m)
            ffn(3)


def _blocks(w, order=None):
    k, m = w.shape
    return w.reshape(k // P, P, m // P, P).transpose(2, 1, 0, 3)


def _pad(b):
    out = np.zeros((b.shape[0], P, TILES, P), np.float32)
    out[:, :, :b.shape[2]] = b
    return out


def _ffn_blocks(w_in, w_out):
    w = _blocks(w_in)
    yield np.stack([w[:KF], w[KF:]], axis=1).reshape(2 * KF, P, TILES, P)
    w = _blocks(w_out)
    parts = [_pad(w[:, :, TILES * i:TILES * (i + 1)]) for i in range(3)]
    yield np.stack(parts, axis=1).reshape(3 * KD, P, TILES, P)


def _weights(v):
    yield from _ffn_blocks(v["ffn1_w_in"][0], v["ffn1_w_out"][0])
    w = _blocks(v["w_in"][0])
    q, k, g, p, gates = w[0:8], w[8:16], w[24:32], w[32:40], w[40:56]
    yield p
    wv = v["w_in"][0][:, 2 * D:3 * D].reshape(4, 2, P, 2, S)
    yield wv.transpose(3, 0, 2, 1, 4).reshape(8, P, TILES, P)
    pw = v["pool_w"][0].reshape(4, 2, P, 2, P).transpose(0, 2, 1, 3, 4).reshape(4, P, 4, P)
    yield _pad(pw)
    yield np.stack([gates[8:], _blocks(v["w_pool_up"][0])], axis=1).reshape(16, P, TILES, P)
    for i in range(HEADS):
        yield from (q[2 * i:2 * i + 2], k[2 * i:2 * i + 2], g[2 * i:2 * i + 2])
    yield np.stack([gates[:8], _blocks(v["w_ret_up"][0])], axis=1).reshape(16, P, TILES, P)
    yield _blocks(v["w_out"][0])
    yield from _ffn_blocks(v["ffn2_w_in"][0], v["ffn2_w_out"][0])
    yield from _ffn_blocks(v["ffn1_w_in_2"][0], v["ffn1_w_out_2"][0])
    w = _blocks(v["w_mix_in_2"][0][:, :28 * P])
    b, c, hh, q, k, vv, z = (w[4 * i:4 * i + 4] for i in range(7))
    yield np.stack([q, k, vv], axis=1).reshape(12, P, TILES, P)
    yield z
    yield np.stack([c, hh, b], axis=1).reshape(12, P, TILES, P)
    yield _blocks(v["w_mix_out_2"][0])
    yield from _ffn_blocks(v["ffn2_w_in_2"][0], v["ffn2_w_out_2"][0])


def _vectors(v):
    def tall(a):
        a = a.reshape(-1, a.shape[-1] // P, P) if a.ndim > 1 else a.reshape(1, -1, P)
        return a.reshape(-1, P).T
    cols = []
    for name in list(VEC)[:14]:
        a = v[name]
        a = a.reshape(-1, a.shape[-1])
        cols.append(tall(a))
    cols.append(np.broadcast_to(v["gdn_A_log_2"].reshape(1, 4), (P, 4)))
    cols.append(np.broadcast_to(v["gdn_dt_bias_2"].reshape(1, 4), (P, 4)))
    ab = v["w_mix_in_2"][0][:, 28 * P:]
    cols.append(ab.reshape(KD, P, 8).transpose(1, 0, 2).reshape(P, 64))
    return np.ascontiguousarray(np.concatenate(cols, axis=1))


def _constants():
    f = np.float32
    p, i = np.arange(P)[:, None], np.arange(P)[None, :]
    edge = [w / np.minimum(np.arange(PADP) + 1.0, w) / w for w in POOL]
    c0 = np.concatenate([np.ones((P, P)), p == i, np.full((P, 1), EPS), np.ones((P, 1)),
                         np.broadcast_to(np.concatenate(edge), (P, 4 * PADP))], axis=1).astype(f)
    half = P
    freq = (f(10000.0) ** (-np.arange(half, dtype=f) / f(half))).astype(f)
    angle = (np.arange(S, dtype=f)[None, :] * freq[:, None]).astype(f)
    s, t = np.arange(P)[:, None], np.arange(S)[None, :]
    decay = []
    for hd in range(HEADS):
        gamma = 1.0 - 2.0 ** (-5.0 - hd)
        same = (s // 64) == (t // 64)
        d = np.where(same, gamma ** np.abs(t - s), np.where(t // 64 > s // 64, gamma ** np.maximum(t - s, 0), 0.0))
        decay.append(d * DK ** -0.5)
    c1 = np.concatenate([np.cos(angle.astype(np.float64)), np.sin(angle.astype(np.float64))] + decay, axis=1).astype(f)
    levels = [(p >> (k + 1) == i >> (k + 1)) & ((p >> k) & 1 == 1) & ((i >> k) & 1 == 0) for k in range(LEVELS)]
    c2 = np.concatenate([p <= i, p >= i, p > i, p // 64 == i // 64, levels[0]] + [m.T for m in levels],
                        axis=1).astype(f)
    return c0, c1, c2


def kernel(**inputs):
    import concourse.bacc as bacc
    from concourse.bass_utils import run_bass_kernel_spmd

    v = {name: np.asarray(a) for name, a in inputs.items()}
    c0, c1, c2 = _constants()
    arrays = {
        "weights": np.concatenate(list(_weights(v))).reshape(NB, P, TILES * P),
        "x_t": np.ascontiguousarray(v["x"][0].T.reshape(KD, P, S).transpose(1, 0, 2)),
        "vectors": _vectors(v), "const0": c0, "const1": c1, "const2": c2,
    }
    nc = bacc.Bacc("TRN2", target_bir_lowering=False, num_devices=1)
    args = [nc.dram_tensor(name, a.shape, F32, kind="ExternalInput").ap() for name, a in arrays.items()]
    out = nc.dram_tensor("y_t", (P, KD, S), F32, kind="ExternalOutput").ap()
    build(nc, *args, out)
    r = run_bass_kernel_spmd(nc, [arrays], core_ids=[0])
    y = r.results[0]["y_t"]
    return np.ascontiguousarray(y.transpose(1, 0, 2).reshape(D, S).T)[None]
```

```python
from contextlib import ExitStack

import numpy as np

import concourse.bass as bass
from concourse import mybir

F32 = mybir.dt.float32
F32R = mybir.dt.float32r
ALU = mybir.AluOpType
ACT = mybir.ActivationFunctionType

P = 128
S = 512
D = 1024
KD = D // P
FF = 2816
KF = FF // P
EPS = 1e-6
NT = S // P
HEADS = 4
DK = 256
W2 = 128
POOL = (2, 4, 8, 16)
PADP = 16
SLOTS = 4
LIMIT = 211968
LEAD = 2
TILES = 8

PHASES = [("ffn0_in", 2 * KF), ("ffn0_out", 3 * KD), ("pool_in", 8), ("v", 8), ("pool_mix", 4),
          ("pool_up", 16), ("heads", 24), ("ret_up", 16), ("mix_out", 8), ("ffn1_in", 2 * KF), ("ffn1_out", 3 * KD),
          ("ffn2_in", 2 * KF), ("ffn2_out", 3 * KD), ("gdn_qkv", 12), ("conv", 12), ("gdn_gate", 4),
          ("mix2_out", 8), ("ffn3_in", 2 * KF), ("ffn3_out", 3 * KD)]
FIRST, NB = {}, 0
for _name, _count in PHASES:
    FIRST[_name] = NB
    NB += _count
OUT0, _n = {}, 0
for _name, _count in PHASES:
    OUT0[_name] = _n
    _n += {"ffn0_out": 8, "ffn1_out": 8, "ffn2_out": 8, "ffn3_out": 8, "pool_mix": 8}.get(_name, _count)

GATED = [("gate", 0)] + [x for m in range(KD - 1) for x in (("gate", m + 1), ("up", m))] + [("up", KD - 1)]

MIX2 = 28


def _plan():
    plan = {}

    def put(slot, stage, *args):
        plan.setdefault(slot, []).append((stage, args))

    for i in range(8):
        put(4 * (i + 3) + 1, "l2_sum", i)
    put(26, "batch_root", 0)
    put(42, "batch_root", 1)
    for i, slot in enumerate([29, 32, 35, 38, 44, 45, 46, 47]):
        put(slot, "l2_norm", i)
    put(28, "decays")
    for i in range(HEADS):
        put([34, 40, 49, 51][i], "turn_k", i)
        put([43, 48, 53, 55][i], "turn_v", i)
    for c, (rows, products, turned) in enumerate([(37, 49, 52), (41, 50, 53), (58, 62, 66), (67, 70, 73)]):
        put(rows, "rows", c)
        put(products, "products", c)
        put(turned, "turn_l", c)
    for i in range(5):
        put([4, 5, 6, 7, 10][i], "ab", i)
    for pair, start in enumerate([56, 75]):
        for k in range(1, 8):
            at = start + 3 * (k - 1)
            if k < 7:
                put(at, "first", 2 * pair, k)
            if k > 1:
                put(at, "second", 2 * pair + 1, k - 1)
            if k < 7:
                put(at + 1, "first", 2 * pair + 1, k)
                put(at + 2, "second", 2 * pair, k)
    for c, slot in enumerate([75, 81, 95, 100]):
        gap = 1 if c == 2 else 2
        put(slot, "read_state", c)
        put(slot + gap, "new_values", c)
        put(slot + 2 * gap + (c == 2), "outputs", c)
    for i in range(4):
        put(4 * (15 + 3 * i) + 1, "conv_square", i)
        put(4 * (15 + 3 * i) + 3, "conv_sum", i)
        put(4 * (16 + 3 * i) + 2, "conv_norm", i)
    for i in range(HEADS):
        put(106 + i // 2, "out_sum", i)
    put(108, "batch_root", 2)
    for i in range(2):
        put(110 + i, "out_norm", i)
    return plan


PLAN = _plan()

VEC = {}
NV = 0
for _name, _n2 in [("norm_ffn1", 8), ("norm_mix", 8), ("gate_bias", 16), ("pool_scale", 8), ("norm_ffn2", 8),
                   ("norm_final", 8), ("ffn1_norm_2", 8), ("mix_norm_2", 8), ("conv_short_w_2", 12),
                   ("conv_out_norm_2", 4), ("gdn_conv_w_2", 48), ("gdn_out_norm_2", 1), ("ffn2_norm_2", 8),
                   ("final_norm_2", 8), ("A_log", 4), ("dt_bias", 4), ("w_ab", 64)]:
    VEC[_name] = NV
    NV += _n2
C_ONES, C_IDENT, C_EPS, C_ONE, C_EDGE = 0, 128, 256, 257, 258
NC0 = C_EDGE + 4 * PADP
C_COS, C_SIN, C_DECAY = 0, S, 2 * S
NC1 = 6 * S
C_TRI, C_CAUSAL, C_STRICT, C_GROUP, C_LEVEL = 0, 128, 256, 384, 512
LEVELS = 7
NC2 = C_LEVEL + (LEVELS + 1) * P


def build(nc, weights, x_t, vectors, const0, const1, const2, out):
    with ExitStack() as ctx:
        top = [0]

        def sbuf_at(name, offset, shape, dt=F32):
            with ExitStack() as c:
                if offset:
                    c.enter_context(nc.sbuf_tensor(name + "_below", [P, offset // 4], F32))
                t = c.enter_context(nc.sbuf_tensor(name, [P] + list(shape), dt))
            size = 4 * int(np.prod(shape))
            top[0] = max(top[0], offset + size)
            return t, offset + (size + 31) // 32 * 32

        def sem(name):
            return ctx.enter_context(nc.semaphore(name))

        at = 0
        h, at = sbuf_at("h", at, [KD, S])
        x_hi, at = sbuf_at("x_hi", at, [KD, S], F32R)
        x_lo, at = sbuf_at("x_lo", at, [KD, S], F32R)
        w_raw, _ = sbuf_at("w_raw", at, [SLOTS, TILES * P])
        w_lo, at = sbuf_at("w_lo", at, [SLOTS, TILES * P], F32R)
        w_hi, at = sbuf_at("w_hi", at, [SLOTS, TILES * P], F32R)
        square, at = sbuf_at("square", at, [2, S])
        sumsq, at = sbuf_at("sumsq", at, [S])
        ident_r, at = sbuf_at("ident_r", at, [P], F32R)
        root, at = sbuf_at("root", at, [8])
        inv_hi, at = sbuf_at("inv_hi", at, [8], F32R)
        inv_lo, at = sbuf_at("inv_lo", at, [8], F32R)
        inv, at = sbuf_at("inv", at, [8])
        rstd, at = sbuf_at("rstd", at, [S])
        vec, at = sbuf_at("vec", at, [NV])
        cst, at = sbuf_at("cst", at, [NC0])
        rtok, at = sbuf_at("rtok", at, [8])
        arena = at
        hid_hi, a = sbuf_at("hid_hi", arena, [KF, S], F32R)
        hid_lo, a = sbuf_at("hid_lo", a, [KF, S], F32R)
        f_gate, a = sbuf_at("f_gate", a, [2, S])
        f_sig, a = sbuf_at("f_sig", a, [2, S])
        f_mul, a = sbuf_at("f_mul", a, [2, S])
        f_hid, a = sbuf_at("f_hid", a, [2, S])
        r_first, b = sbuf_at("r_first", a, [8])
        sumsq2, b = sbuf_at("sumsq2", b, [S])
        r_one, b = sbuf_at("r_one", b, [S])
        square2, b = sbuf_at("square2", b, [2, S])
        assert b <= LIMIT
        pooled_hi, half = sbuf_at("pooled_hi", arena, [KD, S], F32R)
        pooled_lo, b = sbuf_at("pooled_lo", half, [KD, S], F32R)
        merged1, half = sbuf_at("merged1", arena, [KD, S])
        qk, a = sbuf_at("qk", half, [4, S])
        r_raw, a = sbuf_at("r_raw", a, [2, S])
        silu_g, a = sbuf_at("silu_g", a, [2, S])
        assert a == b
        merged_hi, a = sbuf_at("merged_hi", half, [KD, S], F32R)
        merged_lo, b = sbuf_at("merged_lo", a, [KD, S], F32R)
        v_tok, a = sbuf_at("v_tok", a, [NT, D])
        mix_hi, a = sbuf_at("mix_hi", a, [KD, S], F32R)
        mix_lo, a = sbuf_at("mix_lo", a, [KD, S], F32R)
        p_raw, b = sbuf_at("p_raw", a, [2, PADP + S])
        p_sum, b = sbuf_at("p_sum", b, [2, PADP + S])
        p_out, pool_end = sbuf_at("p_out", b, [2, S])
        scored, b = sbuf_at("scored", a, [S + 384 + 256 + 128])
        rot, b = sbuf_at("rot", b, [4, S])
        m_tmp, b = sbuf_at("m_tmp", max(pool_end, b), [2, S])
        m_sig, b = sbuf_at("m_sig", b, [2, S])
        k1c, b = sbuf_at("k1c", b, [NC1])
        final_hi, a = sbuf_at("final_hi", arena, [4, S], F32R)
        tail_a, _ = sbuf_at("tail_a", a - 2 * 4 * S, [2, S])
        tail_b, _ = sbuf_at("tail_b", a + 2 * 4 * S, [2, S])
        final_lo, a = sbuf_at("final_lo", a, [4, S], F32R)
        k2c, a = sbuf_at("k2c", a, [NC2])
        q_t, a = sbuf_at("q_t", a, [HEADS, S])
        v_tk, a = sbuf_at("v_tk", a, [NT, HEADS, W2])
        x_and_l, _ = sbuf_at("x_and_l", a, [NT, HEADS, P])
        o_t, a = sbuf_at("o_t", a, [HEADS, S])
        x_and_l2, _ = sbuf_at("x_and_l2", a, [NT, HEADS, P])
        z_t, a = sbuf_at("z_t", a, [HEADS, S])
        y_inv_t, a = sbuf_at("y_inv_t", a, [NT, HEADS, P])
        gdn_hi, _ = sbuf_at("gdn_hi", a, [HEADS, S], F32R)
        k_t, a = sbuf_at("k_t", a, [HEADS, S])
        gdn_lo, _ = sbuf_at("gdn_lo", a, [HEADS, S], F32R)
        k_tk, a = sbuf_at("k_tk", a, [NT, HEADS, W2])
        at_t, a = sbuf_at("at_t", a, [NT, HEADS, P])
        small, a = sbuf_at("small", a, [16 * 16])
        w_ab, a = sbuf_at("w_ab", a, [KD, 8])
        c_raw, a = sbuf_at("c_raw", a, [2, 4 + S])
        c_acc, a = sbuf_at("c_acc", a, [2, S])
        c_sig, a = sbuf_at("c_sig", a, [2, S])
        c_gate, a = sbuf_at("c_gate", a, [2, S])
        c_y, a = sbuf_at("c_y", a, [2, S])
        v_t = c_y
        state, a = sbuf_at("state", a, [HEADS, W2])
        batch_root, a = sbuf_at("batch_root", a, [48])
        batch_inv, a = sbuf_at("batch_inv", a, [48])
        batch_hi, a = sbuf_at("batch_hi", a, [48], F32R)
        batch_lo, a = sbuf_at("batch_lo", a, [48], F32R)
        lane1, a = sbuf_at("lane1", a, [2, HEADS, P])
        assert a <= LIMIT

        def tile_of(t, i):
            return t[:, i, :].rearrange("p (h n) -> p h n", h=HEADS)

        l_t = [x_and_l[:, 0], x_and_l[:, 2], x_and_l2[:, 0], x_and_l2[:, 2]]
        x_inv = [x_and_l[:, 1], x_and_l[:, 3], x_and_l2[:, 1], x_and_l2[:, 3]]
        level_m = [tile_of(tail_a, 1), lane1[:, 0]]
        level_p = [tile_of(tail_b, 1), lane1[:, 1]]
        carry = sumsq[:, :].rearrange("p (h n) -> p h n", h=HEADS)
        decay_e = [tile_of(tail_a, 0), x_and_l2[:, 0], tile_of(tail_a, 0), tile_of(tail_a, 0)]
        decay_a = [tile_of(tail_b, 0), x_and_l2[:, 1], tile_of(tail_b, 0), tile_of(tail_b, 0)]
        row_exp = [carry, x_and_l2[:, 2], carry, carry]

        acc = [ctx.enter_context(nc.psum_tensor(f"acc{i}", [P, S], F32)) for i in range(4)]
        sums = ctx.enter_context(nc.psum_tensor("sums", [P, S], F32))
        mixb = [ctx.enter_context(nc.psum_tensor(f"mixb{i}", [P, S], F32)) for i in range(3)]

        ones, ident = cst[:, C_ONES:C_ONES + P], cst[:, C_IDENT:C_IDENT + P]
        eps, one = cst[:, C_EPS:C_EPS + 1], cst[:, C_ONE:C_ONE + 1]

        def vcol(name, j, n=1):
            return vec[:, VEC[name] + j:VEC[name] + j + n]

        SMALL = ["g", "beta", "z", "nz", "u", "w", "lnw", "eq", "d", "cum", "total", "e_cum", "e_left", "e_total",
                 "neg_a", "ab4"]

        def sm(name):
            i = 16 * SMALL.index(name)
            return small[:, i:i + 16]

        def per_head(name, c):
            i = 16 * SMALL.index(name) + 4 * c
            return small[:, i:i + 4].unsqueeze(2).to_broadcast([P, HEADS, P])

        def over_heads(column):
            return k2c[:, column:column + P].unsqueeze(1).to_broadcast([P, HEADS, P])

        ident_h = cst[:, C_IDENT:C_IDENT + P].unsqueeze(1).to_broadcast([P, HEADS, P])

        def bank_h(bank):
            return bank[:, :].rearrange("p (h n) -> p h n", h=HEADS)

        def scored_at(i):
            return i * S - P * (i * (i - 1) // 2)

        x_loaded = [sem(f"x_loaded{i}") for i in range(4)]
        tables_loaded = sem("tables_loaded")
        cst_loaded = sem("cst_loaded")
        k1_loaded = sem("k1_loaded")
        k2_loaded = sem("k2_loaded")
        loaded = [sem(f"loaded{i}") for i in range(SLOTS)]
        hi_split = sem("hi_split")
        lo_split = sem("lo_split")
        block_done = sem("block_done")
        drained = sem("drained")
        sq_done = sem("sq_done")
        sq_summed = sem("sq_summed")
        x_hi_done = sem("x_hi_done")
        x_done = sem("x_done")
        summed = sem("summed")
        rooted = sem("rooted")
        inverted = sem("inverted")
        spread = sem("spread")
        inv_used = sem("inv_used")
        ident_done = sem("ident_done")
        f_sig_done = sem("f_sig_done")
        f_step = sem("f_step")
        f_mul_done = sem("f_mul_done")
        hid_hi_done = sem("hid_hi_done")
        hid_done = sem("hid_done")
        chained = sem("chained")
        sq2_done = sem("sq2_done")
        sq2_summed = sem("sq2_summed")
        h_chain = sem("h_chain")
        h_final = sem("h_final")
        zeroed = sem("zeroed")
        dve_step = sem("dve_step")
        pool_step = sem("pool_step")
        act_step = sem("act_step")
        pool_out_done = sem("pool_out_done")
        pooled_hi_done = sem("pooled_hi_done")
        pooled_done = sem("pooled_done")
        m_sig_done = sem("m_sig_done")
        mix_hi_done = sem("mix_hi_done")
        mix_done = sem("mix_done")
        rotated = sem("rotated")
        g_ready = sem("g_ready")
        scores_done = sem("scores_done")
        weighted = sem("weighted")
        av_done = sem("av_done")
        ret_copied = sem("ret_copied")
        ret_normed = sem("ret_normed")
        ret_gated = sem("ret_gated")
        merged_sum = sem("merged_sum")
        merged_hi_done = sem("merged_hi_done")
        merged_done = sem("merged_done")
        y_ready = sem("y_ready")
        stored = sem("stored")
        ab_done = sem("ab_done")
        wab_done = sem("wab_done")
        ab_copied = sem("ab_copied")
        ab_ready = sem("ab_ready")
        ab_act = sem("ab_act")
        g_cum = sem("g_cum")
        conv_done = sem("conv_done")
        conv_sig = sem("conv_sig")
        conv_act = sem("conv_act")
        c_gated = sem("c_gated")
        c_conv = sem("c_conv")
        c_prod = sem("c_prod")
        c_sq = sem("c_sq")
        c_hi = sem("c_hi")
        c_split = sem("c_split")
        z_sig = sem("z_sig")
        z_ready = sem("z_ready")
        batch_sq = sem("batch_sq")
        batch_summed = sem("batch_summed")
        batch_rooted = sem("batch_rooted")
        batch_inverted = sem("batch_inverted")
        batch_spread = sem("batch_spread")
        batch_used = sem("batch_used")
        k_turned = sem("k_turned")
        k_copied = sem("k_copied")
        v_turned = sem("v_turned")
        v_copied = sem("v_copied")
        m_ready = [sem(f"m_ready{i}") for i in range(2)]
        p_done = [sem(f"p_done{i}") for i in range(2)]
        p_copied = [sem(f"p_copied{i}") for i in range(2)]
        xp_done = [sem(f"xp_done{i}") for i in range(2)]
        yp_done = [sem(f"yp_done{i}") for i in range(2)]
        x_step = [sem(f"x_step{i}") for i in range(2)]
        y_step = [sem(f"y_step{i}") for i in range(2)]
        row_done = sem("row_done")
        diff_done = sem("diff_done")
        exp_done = sem("exp_done")
        decay_ready = sem("decay_ready")
        kk_done = sem("kk_done")
        ld_done = sem("ld_done")
        l_done = sem("l_done")
        lt_turned = sem("lt_turned")
        lt_copied = sem("lt_copied")
        x0_done = sem("x0_done")
        q_dec = sem("q_dec")
        k_dec = sem("k_dec")
        ks_done = sem("ks_done")
        r_done = sem("r_done")
        vn_done = sem("vn_done")
        vn_copied = sem("vn_copied")
        os_done = sem("os_done")
        o_copied = sem("o_copied")
        state_done = sem("state_done")
        o_gated = sem("o_gated")
        o_hi = sem("o_hi")
        o_split = sem("o_split")

        def counter(engine, semaphore):
            count = [0]

            def step(instruction):
                count[0] += 1
                instruction.then_inc(semaphore, 1)
                engine.wait_ge(semaphore, count[0])
            return step

        SUM = {}
        for name in (["norm0", "norm1"] + [f"ret{i}" for i in range(HEADS)] + ["norm2", "norm3", "norm3b",
                     "norm4"] + [f"conv{i}" for i in range(4)] + ["norm5", "norm6"]):
            SUM[name] = len(SUM)
        NORM = [("norm_ffn1", None, None), ("norm_mix", "ffn0_out", 0.5), ("norm_ffn2", "mix_out", 1.0),
                ("ffn1_norm_2", "ffn1_out", 0.5), ("mix_norm_2", "ffn2_out", 0.5),
                ("ffn2_norm_2", "mix2_out", 1.0), (None, "ffn3_out", 0.5)]
        FFN_NORM = [0, 2, 3, 5]

        block = ctx.enter_context(nc.Block())

        @block.sync
        def _(sp):
            for i in range(4):
                sp.dma_start(w_raw[:, i, :], weights[i]).then_inc(loaded[i], 16)
                if i == 0:
                    sp.dma_start(vec[:, :], vectors).then_inc(tables_loaded, 16)
                sp.dma_start(h[:, 2 * i:2 * i + 2, :], x_t[:, 2 * i:2 * i + 2, :]).then_inc(x_loaded[i], 16)
                if i == 1:
                    sp.dma_start(cst[:, :], const0).then_inc(cst_loaded, 16)
            with sp.Fori(1, NB // SLOTS) as turn:
                for slot in range(SLOTS):
                    sp.wait_ge(block_done, SLOTS * turn + (slot - SLOTS + 1))
                    sp.dma_start(w_raw[:, slot, :], weights[SLOTS * turn + slot]).then_inc(loaded[slot], 16)
            for m in range(KD):
                sp.wait_ge(y_ready, m + 1)
                sp.dma_start(out[:, m, :], h[:, m, :]).then_inc(stored, 16)
            sp.wait_ge(stored, 16 * KD)

        @block.tensor
        def _(pe):
            def product(slot, j, bank, hi, lo, start, stop):
                w = slice(j * P, (j + 1) * P)
                pe.matmul(bank, w_hi[:, slot, w], hi, start=start, stop=False)
                pe.matmul(bank, w_hi[:, slot, w], lo, start=False, stop=False)
                return pe.matmul(bank, w_lo[:, slot, w], hi, start=False, stop=stop)

            def take_block(n):
                pe.wait_ge(lo_split, n + 1)

            def take_bank(a):
                if a >= 4:
                    pe.wait_ge(drained, a - 3)

            def dense(n, a, hi, lo, middle=None):
                take_block(n)
                take_bank(a)
                for k in range(KD):
                    last = product(n % SLOTS, k, acc[a % 4][:, :], hi[:, k, :], lo[:, k, :], k == 0, k == KD - 1)
                    if k == 3 and middle:
                        middle()
                last.then_inc(block_done, 1)

            def token_sums(name, sources, wait, value, groups=None):
                n = SUM[name]
                pe.wait_ge(wait, value)
                if n:
                    pe.wait_ge(inv_used, n)
                columns = ones[:, 0:1] if groups is None else groups
                width = 1 if groups is None else 2
                for t in range(NT):
                    for i, source in enumerate(sources):
                        last = pe.matmul(sums[:, width * t:width * (t + 1)], source[:, t * P:(t + 1) * P], columns,
                                         start=i == 0, stop=i == len(sources) - 1)
                last.then_inc(summed, 1)

            def spread_inverse(name, groups=False):
                pe.wait_ge(inverted, SUM[name] + 1)
                for t in range(NT):
                    if groups:
                        for g in range(2):
                            half = slice(64 * g, 64 * g + 64)
                            last = pe.matmul(sums[half, t * P:(t + 1) * P],
                                             inv[:, 2 * t + g:2 * t + g + 1].to_broadcast([P, 64]), ident,
                                             start=True, stop=True)
                        continue
                    for part in (inv_hi, inv_lo):
                        r = part[:, t:t + 1].to_broadcast([P, P])
                        last = pe.matmul(sums[:, t * P:(t + 1) * P], r, ident_r[:, :], start=part is inv_hi,
                                         stop=part is inv_lo)
                last.then_inc(spread, 1)

            def ffn(f):
                first, out0 = FIRST[f"ffn{f}_in"], OUT0[f"ffn{f}_in"]
                r = FFN_NORM[f]
                for k in range(KD):
                    pe.wait_ge(x_done, KD * r + k + 1)
                    if k == 0:
                        take_block(first)
                        take_bank(out0)
                    last = product(0, k, acc[0][:, :], x_hi[:, k, :], x_lo[:, k, :], k == 0, k == KD - 1)
                last.then_inc(block_done, 1)
                if f:
                    token_sums(f"norm{r}", [sumsq[:, :]], sq_summed, KD * (r + 1))
                dense(first + 1, out0 + 1, x_hi, x_lo)
                if f:
                    spread_inverse(f"norm{r}")
                else:
                    token_sums("norm0", [sumsq[:, :]], sq_summed, KD)
                if f == 2:
                    token_sums("norm3b", [sumsq2[:, :]], sq2_summed, KD)
                dense(first + 2, out0 + 2, x_hi, x_lo)
                if f == 0 or f == 2:
                    spread_inverse("norm0" if f == 0 else "norm3b")
                dense(first + 3, out0 + 3, x_hi, x_lo)
                with pe.Fori(1, 2 * KF // SLOTS) as i:
                    for b in range(SLOTS):
                        pe.wait_ge(lo_split, SLOTS * i + (first + b + 1))
                        pe.wait_ge(drained, SLOTS * i + (out0 + b - 3))
                        for k in range(KD):
                            last = product(b, k, acc[b][:, :], x_hi[:, k, :], x_lo[:, k, :], k == 0, k == KD - 1)
                        last.then_inc(block_done, 1)
                first, out0 = FIRST[f"ffn{f}_out"], OUT0[f"ffn{f}_out"]
                with pe.Fori(0, KD // 4) as i:
                    for m in range(4):
                        pe.wait_ge(drained, 4 * i + (out0 + m - 3))
                        for part in range(3):
                            b = 3 * m + part
                            pe.wait_ge(lo_split, 12 * i + (first + b + 1))
                            upto = min(KF, TILES * (part + 1))
                            pe.wait_ge(hid_done, KF * f + upto)
                            for k in range(TILES * part, upto):
                                last = product(b % SLOTS, k - TILES * part, acc[m][:, :], hid_hi[:, k, :],
                                               hid_lo[:, k, :], k == 0, k == KF - 1)
                            last.then_inc(block_done, 1)

            def gated_mix(phase, hi, lo, wait, value):
                first, out0 = FIRST[phase], OUT0[phase]
                for j, (kind, m) in enumerate(GATED):
                    if kind == "gate":
                        if phase == "ret_up" and m == 0:
                            tail = f"ret{HEADS - 1}"
                            dense(first, out0, x_hi, x_lo, middle=lambda: token_sums(
                                tail, [square[:, 0, :], square[:, 1, :]], ret_copied, 2 * HEADS))
                            spread_inverse(tail)
                        else:
                            dense(first + j, out0 + j, x_hi, x_lo)
                    else:
                        if m == 0:
                            pe.wait_ge(wait, value)
                        dense(first + j, out0 + j, hi, lo)

            emptied = {}

            def take(bank, semaphore, value):
                if bank in emptied:
                    pe.wait_ge(*emptied[bank])
                emptied[bank] = (semaphore, value)
                return mixb[bank]

            def batch_sum(i):
                pe.wait_ge(batch_sq, i + 1)
                for t in range(NT):
                    col = 4 * i + t
                    last = pe.matmul(sums[:, col:col + 1], square[:, i % 2, t * P:(t + 1) * P], ones[:, 0:1],
                                     start=True, stop=True)
                last.then_inc(batch_summed, 1)

            def batch_spread_out(i, bank):
                pe.wait_ge(batch_inverted, i // 4 + 1)
                for t in range(NT):
                    for part in (batch_hi, batch_lo):
                        r = part[:, 4 * i + t:4 * i + t + 1].to_broadcast([P, P])
                        last = pe.matmul(bank[:, t * P:(t + 1) * P], r, ident_r[:, :], start=part is batch_hi,
                                         stop=part is batch_lo)
                last.then_inc(batch_spread, 1)

            def l2_sum(i):
                if i == 0:
                    pe.wait_ge(inv_used, SUM["norm4"] + 1)
                if i == 4:
                    pe.wait_ge(batch_rooted, 1)
                batch_sum(i)

            def l2_norm(i):
                batch_spread_out(i, take(i % 3, batch_used, i + 1))

            def ab(part):
                if part == 0:
                    take(0, ab_copied, 1)
                    pe.wait_ge(wab_done, 1)
                if part < 4:
                    for k in (2 * part, 2 * part + 1):
                        last = pe.matmul(mixb[0][0:8, :], w_ab[:, k, :], h[:, k, :], start=k == 0, stop=k == KD - 1)
                    if part == 3:
                        last.then_inc(ab_done, 1)
                else:
                    bank = take(1, ab_ready, 1)
                    pe.wait_ge(ab_copied, 1)
                    for t in range(NT):
                        last = pe.transpose(bank[:, 8 * t:8 * t + 8], c_gate[0:8, 0, t * P:(t + 1) * P], ident[0:8, 0:8])
                    last.then_inc(ab_done, 1)

            def decays():
                bank = take(0, ab_act, 2)
                pe.wait_ge(g_cum, 1)
                pe.wait_ge(k2_loaded, 16)
                pe.matmul(bank[:, 0:16], k2c[:, C_TRI:C_TRI + P], sm("g"), start=True, stop=True)
                pe.matmul(bank[:, 16:32], ones, sm("g"), start=True, stop=True).then_inc(ab_done, 1)

            def turn_k(hd):
                bank = take(1, k_copied, hd + 1)
                pe.wait_ge(batch_used, 2 * hd + 2)
                for t in range(NT):
                    last = pe.transpose(bank[:, t * P:(t + 1) * P], k_t[:, hd, t * P:(t + 1) * P], ident)
                last.then_inc(k_turned, 1)

            def turn_v(hd):
                bank = take(2, v_copied, hd + 1)
                pe.wait_ge(conv_act, 2 * HEADS + hd + 1)
                for t in range(NT):
                    last = pe.transpose(bank[:, t * P:(t + 1) * P], v_t[:, hd % 2, t * P:(t + 1) * P], ident)
                last.then_inc(v_turned, 1)

            def rows(c):
                bank = take(0, exp_done, 2 * c + 2)
                for hd in range(HEADS):
                    g = sm("g")[:, 4 * c + hd:4 * c + hd + 1].to_broadcast([P, P])
                    last = pe.matmul(bank[:, hd * P:(hd + 1) * P], g, k2c[:, C_TRI:C_TRI + P], start=True, stop=True)
                last.then_inc(row_done, 1)

            def products(c):
                t = slice(c * P, (c + 1) * P)
                pe.wait_ge(batch_used, 2 * HEADS)
                k_bank, q_bank = take(0, ld_done, 2 * c + 1), take(1, ld_done, 2 * c + 2)
                for hd in range(HEADS):
                    o = slice(hd * P, (hd + 1) * P)
                    pe.matmul(k_bank[:, o], k_t[:, hd, t], k_t[:, hd, t], start=True, stop=True)
                    last = pe.matmul(q_bank[:, o], q_t[:, hd, t], k_t[:, hd, t], start=True, stop=True)
                last.then_inc(kk_done, 1)

            def turn_l(c):
                l_bank, a_bank = take(0, lt_copied, c + 1), take(1, lt_copied, c + 1)
                pe.wait_ge(l_done, c + 1)
                pe.wait_ge(ld_done, 2 * c + 2)
                for hd in range(HEADS):
                    o = slice(hd * P, (hd + 1) * P)
                    pe.transpose(l_bank[:, o], x_inv[c][:, hd, :], ident)
                    last = pe.transpose(a_bank[:, o], decay_a[c][:, hd, :], ident)
                last.then_inc(lt_turned, 1)

            def first(c, k):
                lane, i = c % 2, (LEVELS - 1) * (c // 2) + k
                bank = take(2, p_copied[lane], i)
                pe.wait_ge(m_ready[lane], i)
                if k == 1:
                    pe.wait_ge(x0_done, c + 1)
                else:
                    pe.wait_ge(x_step[lane], (LEVELS - 2) * (c // 2) + k - 1)
                for hd in range(HEADS):
                    last = pe.matmul(bank[:, hd * P:(hd + 1) * P], level_m[lane][:, hd, :], x_inv[c][:, hd, :],
                                     start=True, stop=True)
                last.then_inc(p_done[lane], 1)

            def second(c, k):
                lane, i = c % 2, (LEVELS - 1) * (c // 2) + k
                pe.wait_ge(p_copied[lane], i)
                if k > 1:
                    pe.wait_ge(y_step[lane], i - 1)
                if k < LEVELS - 1:
                    x_bank = take(0, x_step[lane], (LEVELS - 2) * (c // 2) + k)
                    for hd in range(HEADS):
                        last = pe.matmul(x_bank[:, hd * P:(hd + 1) * P], y_inv_t[:, c, hd, :], level_p[lane][:, hd, :],
                                         start=True, stop=True)
                    last.then_inc(xp_done[lane], 1)
                y_bank = take(1, y_step[lane], i)
                for hd in range(HEADS):
                    last = pe.matmul(y_bank[:, hd * P:(hd + 1) * P], level_p[lane][:, hd, :], y_inv_t[:, c, hd, :],
                                     start=True, stop=True)
                last.then_inc(yp_done[lane], 1)

            def read_state(c):
                t = slice(c * P, (c + 1) * P)
                bank = take(0, r_done, c + 1)
                pe.wait_ge(state_done, c + 1)
                pe.wait_ge(y_step[0], (LEVELS - 1) * (c // 2 + 1))
                pe.wait_ge(y_step[1], (LEVELS - 1) * (c // 2 + 1))
                for hd in range(HEADS):
                    last = pe.matmul(bank[:, hd * P:(hd + 1) * P], k_t[:, hd, t], state[:, hd, :],
                                     start=True, stop=True)
                last.then_inc(ks_done, 1)

            def new_values(c):
                bank = take(1, vn_copied, c + 1)
                pe.wait_ge(r_done, c + 1)
                for hd in range(HEADS):
                    last = pe.matmul(bank[:, hd * P:(hd + 1) * P], y_inv_t[:, c, hd, :], v_tk[:, c, hd, :],
                                     start=True, stop=True)
                last.then_inc(vn_done, 1)

            def outputs(c):
                t = slice(c * P, (c + 1) * P)
                o_bank, s_bank = take(2, o_copied, c + 1), take(0, state_done, c + 2)
                pe.wait_ge(vn_copied, c + 1)
                pe.wait_ge(q_dec, c + 1)
                pe.wait_ge(k_dec, c + 1)
                for hd in range(HEADS):
                    o = slice(hd * P, (hd + 1) * P)
                    pe.matmul(o_bank[:, o], state[:, hd, :], q_t[:, hd, t], start=True, stop=False)
                    pe.matmul(o_bank[:, o], v_tk[:, c, hd, :], at_t[:, c, hd, :], start=False, stop=True)
                for hd in range(HEADS):
                    last = pe.matmul(s_bank[:, hd * P:(hd + 1) * P], k_tk[:, c, hd, :], v_tk[:, c, hd, :],
                                     start=True, stop=True)
                last.then_inc(os_done, 1)

            def conv_sum(i):
                token_sums(f"conv{i}", [square[:, i % 2, :]], c_sq, i + 1, k2c[:, C_GROUP:C_GROUP + 2])

            def conv_norm(i):
                spread_inverse(f"conv{i}", groups=True)

            def out_sum(hd):
                if hd == 0:
                    pe.wait_ge(inv_used, SUM["conv3"] + 1)
                batch_sum(2 * HEADS + hd)

            def out_norm(hd):
                i = 2 * HEADS + hd
                batch_spread_out(i, sums if hd == HEADS - 1 else take(hd, batch_used, i + 1))

            stages = dict(ab=ab, l2_sum=l2_sum, l2_norm=l2_norm, decays=decays, turn_k=turn_k, turn_v=turn_v, rows=rows,
                          products=products, turn_l=turn_l, first=first, second=second, read_state=read_state,
                          new_values=new_values, outputs=outputs, conv_sum=conv_sum, conv_norm=conv_norm,
                          out_sum=out_sum, out_norm=out_norm)

            pe.wait_ge(tables_loaded, 16)
            pe.wait_ge(cst_loaded, 16)
            ffn(0)

            n, a = FIRST["pool_in"], OUT0["pool_in"]
            for k in range(KD):
                pe.wait_ge(x_done, KD + k + 1)
                if k == 0:
                    take_block(n)
                    take_bank(a)
                last = product(n % SLOTS, k, acc[a % 4][:, :], x_hi[:, k, :], x_lo[:, k, :], k == 0, k == KD - 1)
            last.then_inc(block_done, 1)
            token_sums("norm1", [sumsq[:, :]], sq_summed, 2 * KD)
            for j in range(1, 8):
                dense(n + j, a + j, x_hi, x_lo)
                if j == 1:
                    spread_inverse("norm1")
            n, a = FIRST["v"], OUT0["v"]
            for half in range(2):
                for part in range(4):
                    b = n + 4 * half + part
                    take_block(b)
                    for kk in range(2):
                        k = 2 * part + kk
                        w = slice(kk * S, (kk + 1) * S)
                        for t in range(NT):
                            x = slice(t * P, (t + 1) * P)
                            if k == 0:
                                take_bank(a + 4 * half + t)
                            pe.matmul(acc[t][:, :], x_hi[:, k, x], w_hi[:, b % SLOTS, w], start=k == 0, stop=False)
                            pe.matmul(acc[t][:, :], x_lo[:, k, x], w_hi[:, b % SLOTS, w], start=False, stop=False)
                            last = pe.matmul(acc[t][:, :], x_hi[:, k, x], w_lo[:, b % SLOTS, w], start=False,
                                             stop=k == KD - 1)
                    last.then_inc(block_done, 1)
            n, a = FIRST["pool_mix"], OUT0["pool_mix"]
            pe.wait_ge(pooled_done, KD)
            for g in range(4):
                take_block(n + g)
                for m in range(2):
                    take_bank(a + 2 * g + m)
                    for k in range(2):
                        last = product((n + g) % SLOTS, 2 * k + m, acc[(a + 2 * g + m) % 4][:, :],
                                       pooled_hi[:, 2 * g + k, :], pooled_lo[:, 2 * g + k, :], k == 0, k == 1)
                last.then_inc(block_done, 1)
            gated_mix("pool_up", mix_hi, mix_lo, drained, OUT0["pool_mix"] + 8)
            n, a = FIRST["heads"], OUT0["heads"]
            for hd in range(HEADS):
                b, o = n + 6 * hd, a + 6 * hd
                for j in range(2):
                    dense(b + j, o + j, x_hi, x_lo)
                if hd:
                    token_sums(f"ret{hd - 1}", [square[:, 0, :], square[:, 1, :]], ret_copied, 2 * hd)
                for j in range(2, 5):
                    dense(b + j, o + j, x_hi, x_lo)
                    if hd and j == 2:
                        spread_inverse(f"ret{hd - 1}")
                pe.wait_ge(rotated, 4 * (hd + 1))
                for i in range(NT):
                    if i >= 2:
                        pe.wait_ge(weighted, 4 * hd + i - 1)
                    elif hd:
                        pe.wait_ge(ret_copied, 2 * hd)
                    for d in range(2):
                        last = pe.matmul(mixb[i % 2][:, 0:S - i * P], qk[:, 2 + d, i * P:(i + 1) * P],
                                         qk[:, d, i * P:S], start=d == 0, stop=d == 1)
                    last.then_inc(scores_done, 1)
                dense(b + 5, o + 5, x_hi, x_lo)
                for e in range(2):
                    pe.wait_ge(weighted, 4 * hd + 4)
                    if e == 0 and hd:
                        pe.wait_ge(ret_copied, 2 * hd - 1)
                    bank = mixb[2] if e == 0 else mixb[0]
                    col = hd * DK + e * P
                    for i in range(NT):
                        off = scored_at(i)
                        last = pe.matmul(bank[:, i * P:S], v_tok[:, i, col:col + P], scored[:, off:off + S - i * P],
                                         start=i == 0, stop=i == NT - 1)
                    last.then_inc(av_done, 1)
            gated_mix("ret_up", mix_hi, mix_lo, mix_done, KD)
            n, a = FIRST["mix_out"], OUT0["mix_out"]
            for m in range(KD):
                if m == 0:
                    pe.wait_ge(merged_done, KD)
                dense(n + m, a + m, merged_hi, merged_lo)
            ffn(1)
            ffn(2)

            n, a = FIRST["gdn_qkv"], OUT0["gdn_qkv"]
            pe.wait_ge(x_done, KD * 5)
            for j in range(MIX2):
                take_block(n + j)
                take_bank(a + j)
                for k in range(KD):
                    last = product((n + j) % SLOTS, k, acc[(a + j) % 4][:, :], x_hi[:, k, :], x_lo[:, k, :],
                                   k == 0, k == KD - 1)
                    if k == KD - 1:
                        last.then_inc(block_done, 1)
                    if k % 2:
                        for stage, args in PLAN.get(4 * j + k // 2, ()):
                            if stage in stages:
                                stages[stage](*args)
                if j == 0:
                    token_sums("norm4", [sumsq[:, :]], sq_summed, 5 * KD)
                if j == 1:
                    spread_inverse("norm4")
            for hd in range(2, HEADS):
                out_norm(hd)
            n, a = FIRST["mix2_out"], OUT0["mix2_out"]
            pe.wait_ge(c_split, 4)
            for part, m in [(0, 0), (0, 1), (0, 2), (1, 0), (1, 1), (1, 2)] + [(p, m) for m in range(3, KD)
                                                                              for p in range(2)]:
                if part == 0:
                    take_block(n + m)
                    take_bank(a + m)
                for i in range(4):
                    if part:
                        pe.wait_ge(o_split, i + 1)
                    hi, lo = (gdn_hi, gdn_lo) if part else (final_hi, final_lo)
                    last = product((n + m) % SLOTS, 4 * part + i, acc[(a + m) % 4][:, :], hi[:, i, :], lo[:, i, :],
                                   4 * part + i == 0, 4 * part + i == KD - 1)
                if part:
                    last.then_inc(block_done, 1)
            ffn(3)
            token_sums("norm6", [sumsq[:, :]], sq_summed, 7 * KD)
            spread_inverse("norm6")


        @block.scalar
        def _(act):
            def split(n):
                if n < NB:
                    slot = n % SLOTS
                    act.wait_ge(loaded[slot], 16 * (n // SLOTS + 1))
                    act.activation(w_hi[:, slot, :], w_raw[:, slot, :], ACT.Copy).then_inc(hi_split, 1)

            def split_in_loop(b, turn):
                slot = b % SLOTS
                act.wait_ge(loaded[slot], 16 * turn + 16 * (b // SLOTS + 1))
                act.activation(w_hi[:, slot, :], w_raw[:, slot, :], ACT.Copy).then_inc(hi_split, 1)

            def residual(r, m):
                gain, phase, _ = NORM[r]
                act.wait_ge(drained, OUT0[phase] + m + 1)
                i = KD * r + m
                if i >= 2:
                    act.wait_ge(sq_summed, i - 1)
                act.activation(square[:, m % 2, :], h[:, m, :], ACT.Square).then_inc(sq_done, 1)
                if r == 3:
                    act.wait_ge(chained, m + 1)
                    if m >= 2:
                        act.wait_ge(sq2_summed, m - 1)
                    act.activation(square2[:, m % 2, :], h[:, m, :], ACT.Square).then_inc(sq2_done, 1)
                if gain:
                    act.activation(x_hi[:, m, :], h[:, m, :], ACT.Copy, scale=vcol(gain, m)).then_inc(x_hi_done, 1)

            def take_root(name, scale, width=4):
                n = SUM[name]
                act.wait_ge(summed, n + 1)
                if n:
                    act.wait_ge(inverted, n)
                act.activation(root[:, 0:width], sums[:, 0:width], ACT.Sqrt, scale=scale, bias=eps).then_inc(rooted, 1)

            def ffn(f):
                first, out0 = FIRST[f"ffn{f}_in"], OUT0[f"ffn{f}_in"]

                def half_pair(b, i, turn, u):
                    if isinstance(i, int):
                        split(first + SLOTS * i + b + LEAD)
                    else:
                        split_in_loop(b + LEAD, turn)

                def turn_of(i):
                    q0 = 2 * i
                    turn = i + first // SLOTS
                    for u in range(2):
                        half_pair(2 * u, i, turn, u)
                        act.wait_ge(drained, 2 * q0 + (out0 + 2 * u + 1))
                        act.activation(f_sig[:, u, :], f_gate[:, u, :], ACT.Sigmoid).then_inc(f_sig_done, 1)
                        half_pair(2 * u + 1, i, turn, u)
                        act.wait_ge(drained, 2 * q0 + (out0 + 2 * u + 2))
                        act.activation(hid_hi[:, q0 + u, :], f_hid[:, u, :], ACT.Copy).then_inc(hid_hi_done, 1)

                r = FFN_NORM[f]
                split(first + LEAD)
                take_root(f"norm{r}", 1.0 / D)
                split(first + 1 + LEAD)
                if f == 2:
                    act.wait_ge(h_chain, 1)
                    act.activation(root[:, 0:4], r_first[:, 4:8], ACT.Sqrt, scale=1.0 / D,
                                   bias=eps).then_inc(rooted, 1)
                for u in range(2):
                    if u:
                        split(first + 2 + LEAD)
                    act.wait_ge(drained, out0 + 2 * u + 1)
                    act.activation(f_sig[:, u, :], f_gate[:, u, :], ACT.Sigmoid).then_inc(f_sig_done, 1)
                    if u:
                        split(first + 2 * u + 1 + LEAD)
                    act.wait_ge(drained, out0 + 2 * u + 2)
                    act.activation(hid_hi[:, u, :], f_hid[:, u, :], ACT.Copy).then_inc(hid_hi_done, 1)
                with act.Fori(1, 2 * KF // SLOTS) as i:
                    turn_of(i)
                first, r = FIRST[f"ffn{f}_out"], [1, 3, 4, 6][f]
                for m in range(KD):
                    for part in range(3):
                        split(first + 3 * m + part + LEAD)
                    residual(r, m)

            def gated_mix(phase, sig0):
                first, out0 = FIRST[phase], OUT0[phase]
                branch = 0 if phase == "ret_up" else 1
                for j, (kind, m) in enumerate(GATED):
                    split(first + j + LEAD)
                    if kind == "gate":
                        if phase == "ret_up" and m == 0:
                            ret_tail_root(HEADS - 1)
                        act.wait_ge(drained, out0 + j + 1)
                        act.activation(m_sig[:, m % 2, :], m_tmp[:, m % 2, :], ACT.Sigmoid,
                                       bias=vcol("gate_bias", KD * branch + m)).then_inc(m_sig_done, 1)
                        if phase == "ret_up" and m == 0:
                            ret_tail_split(HEADS - 1)
                    elif phase == "ret_up":
                        act.wait_ge(merged_sum, m + 1)
                        act.activation(merged_hi[:, m, :], merged1[:, m, :], ACT.Copy).then_inc(merged_hi_done, 1)

            def ret_tail_root(hd):
                take_root(f"ret{hd}", 1.0 / DK)

            def ret_tail_split(hd):
                for e in range(2):
                    act.wait_ge(ret_gated, 2 * hd + e + 1)
                    act.activation(mix_hi[:, 2 * hd + e, :], r_raw[:, e, :], ACT.Copy).then_inc(mix_hi_done, 1)

            split(0)
            act.wait_ge(tables_loaded, 16)
            for m in range(KD):
                act.wait_ge(x_loaded[m // 2], 16)
                act.activation(x_hi[:, m, :], h[:, m, :], ACT.Copy, scale=vcol("norm_ffn1", m)).then_inc(x_hi_done, 1)
            split(1)
            act.wait_ge(cst_loaded, 16)
            act.activation(ident_r[:, :], ident, ACT.Copy).then_inc(ident_done, 1)
            for m in range(KD):
                if m >= 2:
                    act.wait_ge(sq_summed, m - 1)
                act.activation(square[:, m % 2, :], h[:, m, :], ACT.Square).then_inc(sq_done, 1)
            ffn(0)

            n, a = FIRST["pool_in"], OUT0["pool_in"]

            def pooled_split(j):
                act.wait_ge(pool_out_done, j + 1)
                act.activation(pooled_hi[:, j, :], p_out[:, j % 2, :], ACT.Copy).then_inc(pooled_hi_done, 1)

            for j in range(16):
                split(n + j + LEAD)
                if j == 0:
                    take_root("norm1", 1.0 / D)
                if 3 <= j < 3 + KD:
                    pooled_split(j - 3)
            n, a = FIRST["pool_mix"], OUT0["pool_mix"]
            for g in range(4):
                split(n + g + LEAD)
                act.wait_ge(block_done, n + g + 1)
                for m in range(2):
                    j = 2 * g + m
                    act.activation(mix_hi[:, j, :], acc[(a + j) % 4][:, :], ACT.Copy,
                                   scale=vcol("pool_scale", j)).then_inc(mix_hi_done, 1)
            gated_mix("pool_up", 0)
            n, a = FIRST["heads"], OUT0["heads"]
            for hd in range(HEADS):
                b, o = n + 6 * hd, a + 6 * hd
                split(b + LEAD)
                split(b + 1 + LEAD)
                if hd:
                    ret_tail_root(hd - 1)
                split(b + 2 + LEAD)
                split(b + 3 + LEAD)
                if hd:
                    ret_tail_split(hd - 1)
                for e in range(2):
                    split(b + 4 + e + LEAD)
                    act.wait_ge(drained, o + 4 + e + 1)
                    act.activation(m_sig[:, e, :], m_tmp[:, e, :], ACT.Sigmoid).then_inc(m_sig_done, 1)
                for e in range(2):
                    act.wait_ge(av_done, 2 * hd + e + 1)
                    if hd:
                        act.wait_ge(mix_done, 2 * hd - 1 + e)
                    bank = mixb[2] if e == 0 else mixb[0]
                    act.activation(r_raw[:, e, :], bank[:, :], ACT.Copy)
                    act.activation(square[:, e, :], bank[:, :], ACT.Square).then_inc(ret_copied, 1)
            gated_mix("ret_up", 8)
            n, a = FIRST["mix_out"], OUT0["mix_out"]
            for m in range(KD):
                split(n + m + LEAD)
                residual(2, m)
            ffn(1)
            ffn(2)

            n, a = FIRST["gdn_qkv"], OUT0["gdn_qkv"]
            split(n + LEAD)
            take_root("norm4", 1.0 / D)
            split(n + 1 + LEAD)
            step = counter(act, act_step)

            def batch_square(i, src):
                if i >= 2:
                    act.wait_ge(batch_summed, i - 1)
                act.activation(square[:, i % 2, :], src, ACT.Square).then_inc(batch_sq, 1)

            def batch_root_of(i):
                act.wait_ge(batch_summed, 4 * i + 4)
                o = slice(16 * i, 16 * i + 16)
                act.activation(batch_root[:, o], sums[:, o], ACT.Sqrt, scale=1.0 if i < 2 else 1.0 / W2,
                               bias=eps).then_inc(batch_rooted, 1)

            def ab(part):
                if part == 3:
                    act.wait_ge(ab_done, 1)
                    act.activation(c_gate[0:8, 0, :], mixb[0][0:8, :], ACT.Copy).then_inc(ab_copied, 1)

            def decays():
                act.wait_ge(ab_done, 3)
                act.activation(sm("cum"), mixb[0][:, 0:16], ACT.Copy)
                act.activation(sm("total"), mixb[0][:, 16:32], ACT.Copy)
                act.activation(sm("e_cum"), mixb[0][:, 0:16], ACT.Exp)
                act.activation(sm("e_total"), mixb[0][:, 16:32], ACT.Exp).then_inc(ab_act, 1)
                act.wait_ge(ab_ready, 2)
                act.activation(sm("e_left"), sm("e_left"), ACT.Exp).then_inc(ab_act, 1)

            def over_tiles(bank):
                return bank[:, :].rearrange("p (c n) -> p c n", c=NT)

            def turn_k(hd):
                act.wait_ge(k_turned, hd + 1)
                act.activation(k_tk[:, :, hd, :], over_tiles(mixb[1]), ACT.Copy).then_inc(k_copied, 1)

            def turn_v(hd):
                act.wait_ge(v_turned, hd + 1)
                act.activation(v_tk[:, :, hd, :], over_tiles(mixb[2]), ACT.Copy).then_inc(v_copied, 1)

            def rows(c):
                act.wait_ge(diff_done, c + 1)
                act.activation(decay_e[c], decay_e[c], ACT.Exp).then_inc(exp_done, 1)
                if c >= 2:
                    act.wait_ge(q_dec, 1 if c == 2 else 3)
                act.activation(row_exp[c], bank_h(mixb[0]), ACT.Exp).then_inc(exp_done, 1)

            def turn_l(c):
                act.wait_ge(lt_turned, c + 1)
                act.activation(l_t[c], bank_h(mixb[0]), ACT.Copy)
                act.activation(at_t[:, c, :, :], bank_h(mixb[1]), ACT.Copy).then_inc(lt_copied, 1)

            def first_product(c, k):
                lane = c % 2
                act.wait_ge(p_done[lane], (LEVELS - 1) * (c // 2) + k)
                act.activation(level_p[lane], bank_h(mixb[2]), ACT.Copy).then_inc(p_copied[lane], 1)

            def new_values(c):
                act.wait_ge(vn_done, c + 1)
                act.activation(v_tk[:, c, :, :], bank_h(mixb[1]), ACT.Copy).then_inc(vn_copied, 1)

            def outputs(c):
                act.wait_ge(os_done, c + 1)
                act.activation(o_t[:, :, c * P:(c + 1) * P], bank_h(mixb[2]), ACT.Copy).then_inc(o_copied, 1)

            def conv_square(i):
                act.wait_ge(c_prod, i + 1)
                act.activation(square[:, i % 2, :], c_y[:, i % 2, :], ACT.Square).then_inc(c_sq, 1)

            def conv_sum(i):
                take_root(f"conv{i}", 1.0 / 64, 8)

            def conv_norm(i):
                act.wait_ge(inv_used, SUM[f"conv{i}"] + 1)
                if i == 3:
                    act.wait_ge(y_step[0], 2 * (LEVELS - 1))
                act.activation(final_hi[:, i, :], c_y[:, i % 2, :], ACT.Copy).then_inc(c_hi, 1)

            def out_sum(hd):
                if hd == 0:
                    act.wait_ge(o_copied, NT)
                batch_square(2 * HEADS + hd, o_t[:, hd, :])

            def out_norm(hd):
                act.wait_ge(o_gated, hd + 1)
                act.activation(gdn_hi[:, hd, :], o_t[:, hd, :], ACT.Copy).then_inc(o_hi, 1)

            stages = dict(ab=ab, batch_root=batch_root_of, decays=decays, turn_k=turn_k, turn_v=turn_v, rows=rows,
                          turn_l=turn_l, first=first_product, new_values=new_values, outputs=outputs,
                          conv_square=conv_square, conv_sum=conv_sum, conv_norm=conv_norm, out_sum=out_sum,
                          out_norm=out_norm)

            for j in range(MIX2):
                if j >= 2:
                    split(n + j + LEAD)
                for s in range(3):
                    for stage, args in PLAN.get(4 * j + s, ()):
                        if stage in stages:
                            stages[stage](*args)
                if 1 <= j <= 8:
                    i = j - 1
                    act.wait_ge(conv_act, j)
                    batch_square(i, (q_t, k_t)[i % 2][:, i // 2, :])
                if j < 12:
                    act.wait_ge(conv_done, j + 1)
                    act.activation(c_sig[:, j % 2, :], c_acc[:, j % 2, :], ACT.Sigmoid).then_inc(conv_sig, 1)
                elif j >= 24:
                    act.wait_ge(drained, a + j + 1)
                    act.activation(c_sig[:, j % 2, :], c_acc[:, j % 2, :], ACT.Sigmoid).then_inc(z_sig, 1)
                if j == 3:
                    act.wait_ge(ab_ready, 1)
                    act.activation(sm("beta"), sm("beta"), ACT.Sigmoid)
                    act.activation(sm("neg_a")[:, 0:4], vcol("A_log", 0, 4), ACT.Exp)
                    step(act.activation(sm("u"), sm("nz"), ACT.Exp))
                    act.activation(sm("w"), sm("u"), ACT.Copy, bias=1.0)
                    act.activation(sm("lnw"), sm("u"), ACT.Ln, bias=one).then_inc(ab_act, 1)
                for stage, args in PLAN.get(4 * j + 3, ()):
                    if stage in stages:
                        stages[stage](*args)
            n, a = FIRST["mix2_out"], OUT0["mix2_out"]
            split(n + LEAD)
            for hd in range(2, HEADS):
                out_norm(hd)
            for m in range(KD):
                if m:
                    split(n + m + LEAD)
                residual(5, m)
            ffn(3)
            take_root("norm6", 1.0 / D)

        @block.vector
        def _(dve):
            step = counter(dve, dve_step)

            def split(n):
                if n < NB:
                    slot = n % SLOTS
                    dve.wait_ge(hi_split, n + 1)
                    dve.tensor_tensor(w_lo[:, slot, :], w_raw[:, slot, :], w_hi[:, slot, :].bitcast(F32),
                                      ALU.subtract).then_inc(lo_split, 1)

            def residual(r, m):
                gain, phase, scale = NORM[r]
                if phase:
                    a = OUT0[phase] + m
                    first = FIRST[phase]
                    dve.wait_ge(block_done, first + (3 * m + 3 if phase.startswith("ffn") else m + 1))
                    if r == 4 and m == 0:
                        dve.wait_ge(h_final, KD)
                    dve.scalar_tensor_tensor(h[:, m, :], acc[a % 4][:, :], scale, h[:, m, :], ALU.mult,
                                             ALU.add).then_inc(drained, 1)
                if r == 3:
                    dve.wait_ge(sq_done, KD * r + m + 1)
                    dve.tensor_scalar(h[:, m, :], h[:, m, :], vcol("norm_final", m), None,
                                      ALU.mult).then_inc(chained, 1)
                if gain:
                    dve.wait_ge(x_hi_done, KD * [0, 1, 2, 3, 4, 5][r] + m + 1)
                    dve.scalar_tensor_tensor(x_lo[:, m, :], h[:, m, :], vcol(gain, m), x_hi[:, m, :].bitcast(F32),
                                             ALU.mult, ALU.subtract).then_inc(x_done, 1)

            def split_inverse(name, r, width=4):
                step(dve.tensor_copy(inv_hi[:, 0:width], r))
                dve.tensor_tensor(inv_lo[:, 0:width], r, inv_hi[:, 0:width].bitcast(F32),
                                  ALU.subtract).then_inc(inverted, 1)

            def invert(name, r=None, width=4):
                r = inv[:, 0:width] if r is None else r
                dve.wait_ge(rooted, SUM[name] + 1)
                step(dve.reciprocal(r, root[:, 0:width]))
                split_inverse(name, r, width)

            def spread_out(name):
                dve.wait_ge(spread, SUM[name] + 1)

            def keep_inverse(name, out):
                spread_out(name)
                dve.tensor_copy(out, sums[:, :]).then_inc(inv_used, 1)
                dve.wait_ge(inv_used, SUM[name] + 1)

            def ffn(f):
                first, out0 = FIRST[f"ffn{f}_in"], OUT0[f"ffn{f}_in"]
                r = FFN_NORM[f]
                split(first + LEAD)
                invert(f"norm{r}", r_first[:, 0:4] if f == 2 else None)
                split(first + 1 + LEAD)
                keep_inverse(f"norm{r}", r_one[:, :] if f == 2 else rstd[:, :])
                if f == 2:
                    step(dve.tensor_tensor(r_first[:, 4:8], r_first[:, 0:4], r_first[:, 0:4], ALU.mult))
                    dve.wait_ge(summed, SUM["norm3b"] + 1)
                    dve.tensor_tensor(r_first[:, 4:8], sums[:, 0:4], r_first[:, 4:8], ALU.mult).then_inc(h_chain, 1)
                    dve.wait_ge(rooted, SUM["norm3b"] + 1)
                    step(dve.reciprocal(inv[:, 0:4], root[:, 0:4]))
                    step(dve.tensor_tensor(inv[:, 0:4], inv[:, 0:4], r_first[:, 0:4], ALU.mult))
                    split_inverse("norm3b", inv[:, 0:4])
                    keep_inverse("norm3b", rstd[:, :])
                for u in range(2):
                    if u:
                        split(first + 2 * u + LEAD)
                    dve.wait_ge(block_done, first + 2 * u + 1)
                    dve.tensor_tensor(f_gate[:, u, :], acc[2 * u][:, :], rstd[:, :], ALU.mult).then_inc(drained, 1)
                    if u:
                        split(first + 2 * u + 1 + LEAD)
                    dve.wait_ge(block_done, first + 2 * u + 2)
                    dve.wait_ge(f_mul_done, KF * f + u + 1)
                    dve.tensor_tensor(f_hid[:, u, :], acc[2 * u + 1][:, :], f_mul[:, u, :],
                                      ALU.mult).then_inc(drained, 1)
                with dve.Fori(1, 2 * KF // SLOTS) as i:
                    for u in range(2):
                        for b in (2 * u, 2 * u + 1):
                            slot = (b + LEAD) % SLOTS
                            dve.wait_ge(hi_split, SLOTS * i + (first + b + LEAD + 1))
                            dve.tensor_tensor(w_lo[:, slot, :], w_raw[:, slot, :], w_hi[:, slot, :].bitcast(F32),
                                              ALU.subtract).then_inc(lo_split, 1)
                            dve.wait_ge(block_done, SLOTS * i + (first + b + 1))
                            if b % 2 == 0:
                                dve.tensor_tensor(f_gate[:, u, :], acc[b][:, :], rstd[:, :],
                                                  ALU.mult).then_inc(drained, 1)
                            else:
                                dve.wait_ge(f_mul_done, 2 * i + (KF * f + u + 1))
                                dve.tensor_tensor(f_hid[:, u, :], acc[b][:, :], f_mul[:, u, :],
                                                  ALU.mult).then_inc(drained, 1)
                first, r = FIRST[f"ffn{f}_out"], [1, 3, 4, 6][f]
                for m in range(KD):
                    for part in range(3):
                        split(first + 3 * m + part + LEAD)
                    residual(r, m)

            def gated_mix(phase, sig0):
                first, out0 = FIRST[phase], OUT0[phase]
                for j, (kind, m) in enumerate(GATED):
                    split(first + j + LEAD)
                    if phase == "ret_up" and j == 0:
                        invert(f"ret{HEADS - 1}")
                    dve.wait_ge(block_done, first + j + 1)
                    bank = acc[(out0 + j) % 4][:, :]
                    if kind == "gate":
                        if sig0 + m >= 2:
                            dve.wait_ge(m_sig_done, sig0 + m - 1)
                        if phase == "ret_up" and m < 2:
                            dve.wait_ge(g_ready, 2 * HEADS)
                        dve.tensor_tensor(m_tmp[:, m % 2, :], bank, rstd[:, :], ALU.mult).then_inc(drained, 1)
                        if phase == "ret_up" and m == 0:
                            ret_tail_norm(HEADS - 1)
                            ret_tail_split(HEADS - 1)
                        continue
                    dve.wait_ge(m_sig_done, sig0 + m + 1)
                    if phase == "pool_up":
                        dve.tensor_tensor(merged1[:, m, :], bank, m_sig[:, m % 2, :], ALU.mult).then_inc(drained, 1)
                    else:
                        dve.tensor_tensor(m_tmp[:, m % 2, :], bank, m_sig[:, m % 2, :], ALU.mult).then_inc(drained, 1)
                        dve.wait_ge(drained, out0 + j + 1)
                        dve.tensor_tensor(merged1[:, m, :], merged1[:, m, :], m_tmp[:, m % 2, :],
                                          ALU.add).then_inc(merged_sum, 1)
                        dve.wait_ge(merged_hi_done, m + 1)
                        dve.tensor_tensor(merged_lo[:, m, :], merged1[:, m, :], merged_hi[:, m, :].bitcast(F32),
                                          ALU.subtract).then_inc(merged_done, 1)

            def ret_tail_norm(hd):
                spread_out(f"ret{hd}")
                dve.tensor_tensor(r_raw[:, 0, :], r_raw[:, 0, :], sums[:, :], ALU.mult).then_inc(ret_normed, 1)
                dve.tensor_tensor(r_raw[:, 1, :], r_raw[:, 1, :], sums[:, :], ALU.mult).then_inc(inv_used, 1)

            def ret_tail_split(hd):
                for e in range(2):
                    j = 2 * hd + e
                    dve.wait_ge(mix_hi_done, KD + j + 1)
                    dve.tensor_tensor(mix_lo[:, j, :], r_raw[:, e, :], mix_hi[:, j, :].bitcast(F32),
                                      ALU.subtract).then_inc(mix_done, 1)

            split(0)
            dve.wait_ge(tables_loaded, 16)
            for m in range(KD):
                residual(0, m)
            split(1)
            ffn(0)

            n, a = FIRST["pool_in"], OUT0["pool_in"]

            def pooled_split(j):
                dve.wait_ge(pooled_hi_done, j + 1)
                dve.tensor_tensor(pooled_lo[:, j, :], p_out[:, j % 2, :], pooled_hi[:, j, :].bitcast(F32),
                                  ALU.subtract).then_inc(pooled_done, 1)

            for j in range(8):
                if j != 1:
                    split(n + j + LEAD)
                if j == 0:
                    invert("norm1", rtok[:, 0:4])
                    split(n + 1 + LEAD)
                    keep_inverse("norm1", rstd[:, :])
                    dve.wait_ge(zeroed, 1)
                dve.wait_ge(block_done, n + j + 1)
                if j >= 2:
                    dve.wait_ge(pool_out_done, j - 1)
                dve.tensor_tensor(p_raw[:, j % 2, PADP:], acc[(a + j) % 4][:, :], rstd[:, :],
                                  ALU.mult).then_inc(drained, 1)
                if j >= 3:
                    pooled_split(j - 3)
            n, a = FIRST["v"], OUT0["v"]
            for half in range(2):
                for part in range(4):
                    j = 4 * half + part
                    split(n + j + LEAD)
                    if j < 3:
                        pooled_split(5 + j)
                dve.wait_ge(block_done, n + 4 * half + 4)
                for t in range(NT):
                    dve.tensor_scalar(v_tok[:, t, half * S:(half + 1) * S], acc[t][:, :], rtok[:, t:t + 1], None,
                                      ALU.mult).then_inc(drained, 1)
            n, a = FIRST["pool_mix"], OUT0["pool_mix"]
            for g in range(4):
                split(n + g + LEAD)
                for m in range(2):
                    j = 2 * g + m
                    dve.wait_ge(mix_hi_done, j + 1)
                    dve.scalar_tensor_tensor(mix_lo[:, j, :], acc[(a + j) % 4][:, :], vcol("pool_scale", j),
                                             mix_hi[:, j, :].bitcast(F32), ALU.mult, ALU.subtract).then_inc(drained, 1)
            gated_mix("pool_up", 0)
            n, a = FIRST["heads"], OUT0["heads"]
            dve.wait_ge(k1_loaded, 16)
            cos, sin = k1c[:, C_COS:C_COS + S], k1c[:, C_SIN:C_SIN + S]
            step(dve.tensor_tensor(cos, cos, rstd[:, :], ALU.mult))
            step(dve.tensor_tensor(sin, sin, rstd[:, :], ALU.mult))
            for hd in range(HEADS):
                b, o = n + 6 * hd, a + 6 * hd

                def rotate(pair):
                    w = 2 * hd + pair
                    split(b + 2 * pair + LEAD)
                    split(b + 2 * pair + 1 + LEAD)
                    dve.wait_ge(block_done, b + 2 * pair + 2)
                    first, second = (acc[(o + 2 * pair + i) % 4][:, :] for i in range(2))
                    if w:
                        dve.wait_ge(rotated, 2 * w)
                    dve.tensor_tensor(rot[:, 0, :], first, cos, ALU.mult)
                    dve.tensor_tensor(rot[:, 1, :], second, sin, ALU.mult)
                    dve.tensor_tensor(rot[:, 2, :], first, sin, ALU.mult).then_inc(drained, 1)
                    dve.tensor_tensor(rot[:, 3, :], second, cos, ALU.mult).then_inc(drained, 1)

                rotate(0)
                if hd:
                    invert(f"ret{hd - 1}")
                rotate(1)
                if hd:
                    ret_tail_norm(hd - 1)
                    ret_tail_split(hd - 1)
                for e in range(2):
                    split(b + 4 + e + LEAD)
                    dve.wait_ge(block_done, b + 4 + e + 1)
                    if hd:
                        dve.wait_ge(g_ready, 2 * hd - 1 + e)
                    else:
                        dve.wait_ge(m_sig_done, 8)
                    dve.tensor_tensor(m_tmp[:, e, :], acc[(o + 4 + e) % 4][:, :], rstd[:, :],
                                      ALU.mult).then_inc(drained, 1)
                    if e == 0:
                        if hd:
                            dve.wait_ge(av_done, 2 * hd)
                        for i in range(NT):
                            dve.wait_ge(scores_done, 4 * hd + i + 1)
                            off, width = scored_at(i), S - i * P
                            dve.tensor_tensor(scored[:, off:off + width], mixb[i % 2][:, 0:width],
                                              k1c[:, C_DECAY + hd * S:C_DECAY + hd * S + width],
                                              ALU.mult).then_inc(weighted, 1)
            gated_mix("ret_up", 16)
            n, a = FIRST["mix_out"], OUT0["mix_out"]
            for m in range(KD):
                split(n + m + LEAD)
                residual(2, m)
            ffn(1)
            ffn(2)

            n, a = FIRST["gdn_qkv"], OUT0["gdn_qkv"]
            dve.tensor_tensor(w_ab[:, :, :], vcol("w_ab", 0, 64).rearrange("p (k n) -> p k n", k=KD),
                              vcol("mix_norm_2", 0, KD).unsqueeze(2).to_broadcast([P, KD, 8]),
                              ALU.mult).then_inc(wab_done, 1)
            split(n + LEAD)
            invert("norm4", rtok[:, 0:4])
            split(n + 1 + LEAD)
            keep_inverse("norm4", rstd[:, :])
            dve.wait_ge(zeroed, 2)
            token = rtok[:, 0:4].unsqueeze(2).to_broadcast([P, NT, HEADS])

            def ch(name):
                return sm(name).rearrange("p (c n) -> p c n", c=NT)

            def ab(part):
                if part == 4:
                    dve.wait_ge(ab_done, 2)
                    inputs = mixb[1][:, 0:32].rearrange("p (c n) -> p c n", c=NT)
                    dve.tensor_tensor(ch("beta"), inputs[:, :, 0:4], token, ALU.mult)
                    step(dve.tensor_tensor(ch("z"), inputs[:, :, 4:8], token, ALU.mult))
                    step(dve.tensor_tensor(ch("z"), ch("z"),
                                           vcol("dt_bias", 0, 4).unsqueeze(1).to_broadcast([P, NT, HEADS]), ALU.add))
                    dve.scalar_tensor_tensor(sm("nz"), sm("z"), -1.0, sm("z"), ALU.mult,
                                             ALU.min).then_inc(ab_ready, 1)

            def log_decay():
                dve.wait_ge(ab_act, 1)
                step(dve.tensor_scalar(sm("d"), sm("w"), -1.0, None, ALU.add))
                step(dve.tensor_scalar(sm("eq"), sm("d"), 0.0, None, ALU.is_equal))
                dve.tensor_tensor(sm("d"), sm("d"), sm("eq"), ALU.add)
                step(dve.tensor_tensor(sm("lnw"), sm("lnw"), sm("eq"), ALU.add))
                step(dve.reciprocal(sm("d"), sm("d")))
                step(dve.tensor_tensor(sm("lnw"), sm("lnw"), sm("d"), ALU.mult))
                step(dve.tensor_tensor(sm("lnw"), sm("lnw"), sm("u"), ALU.mult))
                step(dve.scalar_tensor_tensor(sm("lnw"), sm("z"), 0.0, sm("lnw"), ALU.max, ALU.add))
                step(dve.tensor_scalar(sm("lnw"), sm("lnw"), -1.0, None, ALU.mult))
                dve.tensor_tensor(ch("g"), ch("lnw"),
                                  sm("neg_a")[:, 0:4].unsqueeze(1).to_broadcast([P, NT, HEADS]),
                                  ALU.mult).then_inc(g_cum, 1)

            def batch_root_of(i):
                o = slice(16 * i, 16 * i + 16)
                dve.wait_ge(batch_rooted, i + 1)
                step(dve.reciprocal(batch_inv[:, o], batch_root[:, o]))
                step(dve.tensor_copy(batch_hi[:, o], batch_inv[:, o]))
                dve.tensor_tensor(batch_lo[:, o], batch_inv[:, o], batch_hi[:, o].bitcast(F32),
                                  ALU.subtract).then_inc(batch_inverted, 1)

            def l2_norm(i):
                hd, kind = i // 2, i % 2
                dve.wait_ge(batch_spread, i + 1)
                dst = (q_t, k_t)[kind][:, hd, :]
                dve.scalar_tensor_tensor(dst, dst, W2 ** -0.5 if kind == 0 else 1.0, mixb[i % 3][:, :], ALU.mult,
                                         ALU.mult).then_inc(batch_used, 1)

            def decays():
                dve.wait_ge(k2_loaded, 16)
                dve.wait_ge(ab_act, 2)
                dve.tensor_tensor(sm("e_left"), sm("total"), sm("cum"), ALU.subtract).then_inc(ab_ready, 1)

            def rows(c):
                dve.wait_ge(row_done, c + 1)
                step(dve.tensor_tensor(decay_e[c], per_head("cum", c), bank_h(mixb[0]), ALU.subtract))
                dve.scalar_tensor_tensor(decay_e[c], decay_e[c], 0.0, over_heads(C_STRICT), ALU.min,
                                         ALU.mult).then_inc(diff_done, 1)

            def products(c):
                dve.wait_ge(decay_ready, c + 1)
                dve.wait_ge(kk_done, c + 1)
                dve.tensor_tensor(x_inv[c], bank_h(mixb[0]), decay_e[c], ALU.mult).then_inc(ld_done, 1)
                dve.tensor_tensor(decay_a[c], bank_h(mixb[1]), decay_e[c], ALU.mult).then_inc(ld_done, 1)

            def turn_l(c):
                dve.wait_ge(lt_turned, c + 1)
                dve.wait_ge(ld_done, 2 * c + 2)
                step(dve.tensor_tensor(decay_e[c], x_inv[c], over_heads(C_LEVEL), ALU.mult))
                step(dve.tensor_tensor(x_inv[c], ident_h, decay_e[c], ALU.subtract))
                dve.wait_ge(lt_copied, c + 1)
                step(dve.tensor_tensor(decay_e[c], l_t[c], over_heads(C_LEVEL + P), ALU.mult))
                dve.tensor_tensor(y_inv_t[:, c, :, :], ident_h, decay_e[c], ALU.subtract).then_inc(x0_done, 1)

            def second(c, k):
                lane, i = c % 2, (LEVELS - 1) * (c // 2) + k
                if k == 1:
                    dve.wait_ge(x0_done, c + 1)
                else:
                    dve.wait_ge(y_step[lane], i - 1)
                if k < LEVELS - 1:
                    dve.wait_ge(xp_done[lane], (LEVELS - 2) * (c // 2) + k)
                    dve.tensor_tensor(x_inv[c], x_inv[c], bank_h(mixb[0]), ALU.subtract).then_inc(x_step[lane], 1)
                dve.wait_ge(yp_done[lane], i)
                dve.tensor_tensor(y_inv_t[:, c, :, :], y_inv_t[:, c, :, :], bank_h(mixb[1]),
                                  ALU.subtract).then_inc(y_step[lane], 1)

            def read_state(c):
                dve.wait_ge(ks_done, c + 1)
                dve.wait_ge(q_dec, NT)
                step(dve.tensor_tensor(carry, bank_h(mixb[0]), per_head("e_cum", c), ALU.mult))
                step(dve.tensor_tensor(v_tk[:, c, :, :], v_tk[:, c, :, :], carry, ALU.subtract))
                dve.tensor_tensor(v_tk[:, c, :, :], v_tk[:, c, :, :], per_head("beta", c), ALU.mult).then_inc(r_done, 1)

            def outputs(c):
                dve.wait_ge(os_done, c + 1)
                step(dve.tensor_tensor(state[:, :, :], state[:, :, :], per_head("e_total", c), ALU.mult))
                dve.tensor_tensor(state[:, :, :], state[:, :, :], bank_h(mixb[0]), ALU.add).then_inc(state_done, 1)

            def conv_sum(i):
                invert(f"conv{i}", width=8)

            def conv_norm(i):
                spread_out(f"conv{i}")
                dve.scalar_tensor_tensor(c_y[:, i % 2, :], c_y[:, i % 2, :], vcol("conv_out_norm_2", i), sums[:, :],
                                         ALU.mult, ALU.mult).then_inc(inv_used, 1)
                dve.wait_ge(c_hi, i + 1)
                dve.tensor_tensor(final_lo[:, i, :], c_y[:, i % 2, :], final_hi[:, i, :].bitcast(F32),
                                  ALU.subtract).then_inc(c_split, 1)

            def out_lo(hd):
                dve.wait_ge(o_hi, hd + 1)
                dve.tensor_tensor(gdn_lo[:, hd, :], o_t[:, hd, :], gdn_hi[:, hd, :].bitcast(F32),
                                  ALU.subtract).then_inc(o_split, 1)

            def out_norm(hd):
                i = 2 * HEADS + hd
                dve.wait_ge(batch_spread, i + 1)
                bank = sums if hd == HEADS - 1 else mixb[hd]
                dve.scalar_tensor_tensor(o_t[:, hd, :], o_t[:, hd, :], vcol("gdn_out_norm_2", 0), bank[:, :], ALU.mult,
                                         ALU.mult).then_inc(batch_used, 1)
                if hd:
                    out_lo(hd - 1)

            stages = dict(ab=ab, batch_root=batch_root_of, l2_norm=l2_norm, decays=decays, rows=rows, products=products,
                          turn_l=turn_l, second=second, read_state=read_state, outputs=outputs, conv_sum=conv_sum,
                          conv_norm=conv_norm, out_norm=out_norm)

            dve.memset(state[:, :, :], 0.0).then_inc(state_done, 1)
            for j in range(MIX2):
                if j >= 2:
                    split(n + j + LEAD)
                for s in range(3):
                    for stage, args in PLAN.get(4 * j + s, ()):
                        if stage in stages:
                            stages[stage](*args)
                dve.wait_ge(block_done, n + j + 1)
                bank = acc[(a + j) % 4][:, :]
                if j < 12:
                    if j >= 2:
                        dve.wait_ge(conv_act, j - 1)
                    u = j % 2
                    dve.tensor_tensor(c_raw[:, u, 4:], bank, rstd[:, :], ALU.mult).then_inc(drained, 1)
                    dve.wait_ge(drained, a + j + 1)
                    channel = HEADS * (j % 2) + j // 2 if j < 8 else j
                    for tap in range(4):
                        w = vcol("gdn_conv_w_2", 12 * tap + channel)
                        src = c_raw[:, u, 1 + tap:1 + tap + S]
                        if tap == 0:
                            step(dve.tensor_scalar(c_acc[:, u, :], src, w, None, ALU.mult))
                        else:
                            ins = dve.scalar_tensor_tensor(c_acc[:, u, :], src, w, c_acc[:, u, :], ALU.mult, ALU.add)
                            if tap == 3:
                                ins.then_inc(conv_done, 1)
                            else:
                                step(ins)
                elif j < 24:
                    i, u = (j - 12) // 3, (j - 12) // 3 % 2
                    if j == 12:
                        dve.wait_ge(conv_act, 12)
                    if j % 3 == 0:
                        dve.tensor_tensor(c_gate[:, u, :], bank, rstd[:, :], ALU.mult).then_inc(drained, 1)
                    elif j % 3 == 1:
                        dve.tensor_tensor(c_sig[:, u, :], bank, rstd[:, :], ALU.mult).then_inc(drained, 1)
                        dve.wait_ge(c_gated, i + 1)
                        for tap in range(3):
                            w = vcol("conv_short_w_2", 4 * tap + i)
                            src = c_raw[:, u, 2 + tap:2 + tap + S]
                            if tap == 0:
                                step(dve.tensor_scalar(c_acc[:, u, :], src, w, None, ALU.mult))
                            else:
                                ins = dve.scalar_tensor_tensor(c_acc[:, u, :], src, w, c_acc[:, u, :], ALU.mult,
                                                               ALU.add)
                                if tap == 1:
                                    step(ins)
                                else:
                                    ins.then_inc(c_conv, 1)
                    else:
                        dve.tensor_tensor(c_gate[:, u, :], bank, rstd[:, :], ALU.mult).then_inc(drained, 1)
                else:
                    if j == 24:
                        dve.wait_ge(c_prod, 4)
                    if j >= 26:
                        dve.wait_ge(z_ready, j - 25)
                    dve.tensor_tensor(c_acc[:, j % 2, :], bank, rstd[:, :], ALU.mult).then_inc(drained, 1)
                if j == 4:
                    log_decay()
                for stage, args in PLAN.get(4 * j + 3, ()):
                    if stage in stages:
                        stages[stage](*args)
            n, a = FIRST["mix2_out"], OUT0["mix2_out"]
            split(n + LEAD)
            for hd in range(2, HEADS):
                out_norm(hd)
            out_lo(HEADS - 1)
            for m in range(KD):
                if m:
                    split(n + m + LEAD)
                residual(5, m)
            ffn(3)
            invert("norm6")
            keep_inverse("norm6", rstd[:, :])
            for m in range(KD):
                dve.scalar_tensor_tensor(h[:, m, :], h[:, m, :], vcol("final_norm_2", m), rstd[:, :], ALU.mult,
                                         ALU.mult).then_inc(y_ready, 1)

        @block.gpsimd
        def _(pool):
            step = counter(pool, pool_step)

            def add_square(r, m):
                i = KD * r + m
                pool.wait_ge(sq_done, i + 1)
                if m == 0:
                    if r:
                        pool.wait_ge(summed, SUM[f"norm{r}"])
                    pool.tensor_copy(sumsq[:, :], square[:, 0, :]).then_inc(sq_summed, 1)
                else:
                    pool.wait_ge(sq_summed, i)
                    pool.tensor_tensor(sumsq[:, :], sumsq[:, :], square[:, m % 2, :], ALU.add).then_inc(sq_summed, 1)
                if r == 3:
                    pool.wait_ge(sq2_done, m + 1)
                    if m == 0:
                        pool.tensor_copy(sumsq2[:, :], square2[:, 0, :]).then_inc(sq2_summed, 1)
                    else:
                        pool.wait_ge(sq2_summed, m)
                        pool.tensor_tensor(sumsq2[:, :], sumsq2[:, :], square2[:, m % 2, :],
                                           ALU.add).then_inc(sq2_summed, 1)

            def ffn(f):
                out0 = OUT0[f"ffn{f}_in"]
                with pool.Fori(0, KF // 2) as i:
                    for u in range(2):
                        q = 2 * i + (KF * f + u)
                        pool.wait_ge(f_sig_done, q + 1)
                        pool.tensor_tensor(f_mul[:, u, :], f_gate[:, u, :], f_sig[:, u, :], ALU.mult).then_inc(f_step, 1)
                        pool.wait_ge(f_step, q + 1)
                        pool.tensor_tensor(f_mul[:, u, :], f_mul[:, u, :], rstd[:, :], ALU.mult).then_inc(f_mul_done, 1)
                        pool.wait_ge(hid_hi_done, q + 1)
                        pool.tensor_tensor(hid_lo[:, 2 * i + u, :], f_hid[:, u, :], hid_hi[:, 2 * i + u, :].bitcast(F32),
                                           ALU.subtract).then_inc(hid_done, 1)
                if f == 2:
                    for m in range(KD):
                        pool.tensor_tensor(h[:, m, :], h[:, m, :], r_one[:, :], ALU.mult).then_inc(h_final, 1)
                r = [1, 3, 4, 6][f]
                for m in range(KD):
                    add_square(r, m)

            for m in range(KD):
                add_square(0, m)
            ffn(0)

            pool.memset(p_raw[:, :, 0:PADP], 0.0)
            pool.memset(p_sum[:, :, 0:PADP], 0.0).then_inc(zeroed, 1)
            pool.wait_ge(summed, SUM["norm1"] + 1)
            pool.dma_start(k1c[:, :], const1).then_inc(k1_loaded, 16)
            pool.wait_ge(zeroed, 1)
            for j in range(8):
                g, u = j // 2, j % 2
                pool.wait_ge(drained, OUT0["pool_in"] + j + 1)
                src, width, to = p_raw[:, u, :], 1, 0
                while width < POOL[g]:
                    step(pool.tensor_tensor(p_sum[:, to, PADP:], src[:, PADP:], src[:, PADP - width:PADP + S - width],
                                            ALU.add))
                    src, width, to = p_sum[:, to, :], 2 * width, 1 - to
                if j >= 2:
                    pool.wait_ge(pooled_done, j - 1)
                step(pool.tensor_scalar(p_out[:, u, :], src[:, PADP:], 1.0 / POOL[g], None, ALU.mult))
                step(pool.tensor_tensor(p_out[:, u, 0:PADP], src[:, PADP:2 * PADP],
                                        cst[:, C_EDGE + g * PADP:C_EDGE + (g + 1) * PADP], ALU.mult))
                pool.tensor_tensor(p_out[:, u, :], p_out[:, u, :], p_raw[:, u, PADP:],
                                   ALU.subtract).then_inc(pool_out_done, 1)
            a = OUT0["heads"]

            def ret_gate(hd):
                for e in range(2):
                    if e == 0:
                        pool.wait_ge(ret_normed, hd + 1)
                    else:
                        pool.wait_ge(inv_used, SUM[f"ret{hd}"] + 1)
                    pool.tensor_tensor(r_raw[:, e, :], r_raw[:, e, :], silu_g[:, e, :], ALU.mult).then_inc(ret_gated, 1)

            for hd in range(HEADS):
                o = a + 6 * hd
                for pair in range(2):
                    pool.wait_ge(drained, o + 2 * pair + 1)
                    pool.tensor_tensor(qk[:, 2 * pair, :], rot[:, 0, :], rot[:, 1, :], ALU.subtract).then_inc(rotated, 1)
                    pool.wait_ge(drained, o + 2 * pair + 2)
                    pool.tensor_tensor(qk[:, 2 * pair + 1, :], rot[:, 2, :], rot[:, 3, :], ALU.add).then_inc(rotated, 1)
                if hd:
                    ret_gate(hd - 1)
                for e in range(2):
                    pool.wait_ge(m_sig_done, 8 + 2 * hd + e + 1)
                    pool.tensor_tensor(silu_g[:, e, :], m_tmp[:, e, :], m_sig[:, e, :], ALU.mult).then_inc(g_ready, 1)
            ret_gate(HEADS - 1)
            for m in range(KD):
                add_square(2, m)
            ffn(1)
            ffn(2)

            pool.memset(c_raw[:, :, 0:4], 0.0).then_inc(zeroed, 1)
            pool.wait_ge(summed, SUM["norm4"] + 1)
            pool.dma_start(k2c[:, :], const2).then_inc(k2_loaded, 16)
            def rows(c):
                pool.wait_ge(exp_done, 2 * c + 1)
                pool.wait_ge(k2_loaded, 16)
                pool.tensor_tensor(decay_e[c], decay_e[c], over_heads(C_CAUSAL), ALU.mult).then_inc(decay_ready, 1)

            def products(c):
                pool.wait_ge(ld_done, 2 * c + 1)
                pool.tensor_tensor(x_inv[c], x_inv[c], per_head("beta", c), ALU.mult).then_inc(l_done, 1)
                t = slice(c * P, (c + 1) * P)
                pool.wait_ge(exp_done, 2 * c + 2)
                pool.wait_ge(ld_done, 2 * c + 2)
                pool.tensor_tensor(q_t[:, :, t], q_t[:, :, t], row_exp[c],
                                   ALU.mult).then_inc(q_dec, 1)

            def first(c, k):
                lane, i = c % 2, (LEVELS - 1) * (c // 2) + k
                pool.wait_ge(lt_copied, c + 1)
                if i > 1:
                    pool.wait_ge(p_done[lane], i - 1)
                pool.tensor_tensor(level_m[lane], l_t[c], over_heads(C_LEVEL + (k + 1) * P),
                                   ALU.mult).then_inc(m_ready[lane], 1)
                if k == 3:
                    pool.wait_ge(ab_act, 3)
                    pool.wait_ge(k_copied, HEADS)
                    pool.tensor_tensor(k_tk[:, c, :, :], k_tk[:, c, :, :], per_head("e_left", c),
                                       ALU.mult).then_inc(k_dec, 1)

            def out_norm(hd):
                pool.wait_ge(batch_used, 2 * HEADS + hd + 1)
                pool.wait_ge(z_ready, hd + 1)
                pool.tensor_tensor(o_t[:, hd, :], o_t[:, hd, :], z_t[:, hd, :], ALU.mult).then_inc(o_gated, 1)

            stages = dict(rows=rows, products=products, first=first, out_norm=out_norm)

            for j in range(MIX2):
                for s in range(3):
                    for stage, args in PLAN.get(4 * j + s, ()):
                        if stage in stages:
                            stages[stage](*args)
                if j < 12:
                    pool.wait_ge(conv_sig, j + 1)
                    if j >= 10:
                        pool.wait_ge(v_turned, j - 9)
                    dst = (q_t, k_t)[j % 2][:, j // 2, :] if j < 8 else v_t[:, j % 2, :]
                    pool.tensor_tensor(dst, c_acc[:, j % 2, :], c_sig[:, j % 2, :], ALU.mult).then_inc(conv_act, 1)
                elif j < 24:
                    i, u = (j - 12) // 3, (j - 12) // 3 % 2
                    pool.wait_ge(drained, OUT0["gdn_qkv"] + j + 1)
                    if j % 3 == 1:
                        pool.tensor_tensor(c_raw[:, u, 4:], c_sig[:, u, :], c_gate[:, u, :], ALU.mult).then_inc(c_gated, 1)
                    elif j % 3 == 2:
                        pool.wait_ge(c_conv, i + 1)
                        if i == 0:
                            pool.wait_ge(v_turned, HEADS)
                        if i >= 2:
                            pool.wait_ge(c_split, i - 1)
                        pool.tensor_tensor(c_y[:, u, :], c_acc[:, u, :], c_gate[:, u, :], ALU.mult).then_inc(c_prod, 1)
                else:
                    hd = j - 24
                    pool.wait_ge(z_sig, hd + 1)
                    if hd == 0:
                        for lane in range(2):
                            pool.wait_ge(y_step[lane], 2 * (LEVELS - 1))
                    pool.tensor_tensor(z_t[:, hd, :], c_acc[:, j % 2, :], c_sig[:, j % 2, :],
                                       ALU.mult).then_inc(z_ready, 1)
                for stage, args in PLAN.get(4 * j + 3, ()):
                    if stage in stages:
                        stages[stage](*args)
            for hd in range(2, HEADS):
                out_norm(hd)
            for m in range(KD):
                add_square(5, m)
            ffn(3)


def _blocks(w, order=None):
    k, m = w.shape
    return w.reshape(k // P, P, m // P, P).transpose(2, 1, 0, 3)


def _pad(b):
    out = np.zeros((b.shape[0], P, TILES, P), np.float32)
    out[:, :, :b.shape[2]] = b
    return out


def _ffn_blocks(w_in, w_out):
    w = _blocks(w_in)
    yield np.stack([w[:KF], w[KF:]], axis=1).reshape(2 * KF, P, TILES, P)
    w = _blocks(w_out)
    parts = [_pad(w[:, :, TILES * i:TILES * (i + 1)]) for i in range(3)]
    yield np.stack(parts, axis=1).reshape(3 * KD, P, TILES, P)


def _gated(gates, up):
    return np.stack([(gates if kind == "gate" else up)[m] for kind, m in GATED])


def _weights(v):
    yield from _ffn_blocks(v["ffn1_w_in"][0], v["ffn1_w_out"][0])
    w = _blocks(v["w_in"][0])
    q, k, g, p, gates = w[0:8], w[8:16], w[24:32], w[32:40], w[40:56]
    yield p
    wv = v["w_in"][0][:, 2 * D:3 * D].reshape(4, 2, P, 2, S)
    yield wv.transpose(3, 0, 2, 1, 4).reshape(8, P, TILES, P)
    pw = v["pool_w"][0].reshape(4, 2, P, 2, P).transpose(0, 2, 1, 3, 4).reshape(4, P, 4, P)
    yield _pad(pw)
    yield _gated(gates[8:], _blocks(v["w_pool_up"][0]))
    for i in range(HEADS):
        yield from (q[2 * i:2 * i + 2], k[2 * i:2 * i + 2], g[2 * i:2 * i + 2])
    yield _gated(gates[:8], _blocks(v["w_ret_up"][0]))
    yield _blocks(v["w_out"][0])
    yield from _ffn_blocks(v["ffn2_w_in"][0], v["ffn2_w_out"][0])
    yield from _ffn_blocks(v["ffn1_w_in_2"][0], v["ffn1_w_out_2"][0])
    w = _blocks(v["w_mix_in_2"][0][:, :28 * P])
    b, c, hh, q, k, vv, z = (w[4 * i:4 * i + 4] for i in range(7))
    yield np.stack([q, k], axis=1).reshape(8, P, TILES, P)
    yield vv
    yield np.stack([c, hh, b], axis=1).reshape(12, P, TILES, P)
    yield z
    yield _blocks(v["w_mix_out_2"][0])
    yield from _ffn_blocks(v["ffn2_w_in_2"][0], v["ffn2_w_out_2"][0])


def _vectors(v):
    def tall(a):
        a = a.reshape(-1, a.shape[-1] // P, P) if a.ndim > 1 else a.reshape(1, -1, P)
        return a.reshape(-1, P).T
    cols = []
    for name in list(VEC)[:14]:
        a = v[name]
        a = a.reshape(-1, a.shape[-1])
        cols.append(tall(a))
    cols.append(np.broadcast_to(v["gdn_A_log_2"].reshape(1, 4), (P, 4)))
    cols.append(np.broadcast_to(v["gdn_dt_bias_2"].reshape(1, 4), (P, 4)))
    ab = v["w_mix_in_2"][0][:, 28 * P:]
    cols.append(ab.reshape(KD, P, 8).transpose(1, 0, 2).reshape(P, 64))
    return np.ascontiguousarray(np.concatenate(cols, axis=1))


def _constants():
    f = np.float32
    p, i = np.arange(P)[:, None], np.arange(P)[None, :]
    edge = [w / np.minimum(np.arange(PADP) + 1.0, w) / w for w in POOL]
    c0 = np.concatenate([np.ones((P, P)), p == i, np.full((P, 1), EPS), np.ones((P, 1)),
                         np.broadcast_to(np.concatenate(edge), (P, 4 * PADP))], axis=1).astype(f)
    half = P
    freq = (f(10000.0) ** (-np.arange(half, dtype=f) / f(half))).astype(f)
    angle = (np.arange(S, dtype=f)[None, :] * freq[:, None]).astype(f)
    s, t = np.arange(P)[:, None], np.arange(S)[None, :]
    decay = []
    for hd in range(HEADS):
        gamma = 1.0 - 2.0 ** (-5.0 - hd)
        same = (s // 64) == (t // 64)
        d = np.where(same, gamma ** np.abs(t - s), np.where(t // 64 > s // 64, gamma ** np.maximum(t - s, 0), 0.0))
        decay.append(d * DK ** -0.5)
    c1 = np.concatenate([np.cos(angle.astype(np.float64)), np.sin(angle.astype(np.float64))] + decay, axis=1).astype(f)
    levels = [(p >> (k + 1) == i >> (k + 1)) & ((p >> k) & 1 == 1) & ((i >> k) & 1 == 0) for k in range(LEVELS)]
    c2 = np.concatenate([p <= i, p >= i, p > i, p // 64 == i % 2, levels[0]] + [m.T for m in levels],
                        axis=1).astype(f)
    return c0, c1, c2


def kernel(**inputs):
    import concourse.bacc as bacc
    from concourse.bass_utils import run_bass_kernel_spmd

    v = {name: np.asarray(a) for name, a in inputs.items()}
    c0, c1, c2 = _constants()
    arrays = {
        "weights": np.concatenate(list(_weights(v))).reshape(NB, P, TILES * P),
        "x_t": np.ascontiguousarray(v["x"][0].T.reshape(KD, P, S).transpose(1, 0, 2)),
        "vectors": _vectors(v), "const0": c0, "const1": c1, "const2": c2,
    }
    nc = bacc.Bacc("TRN2", target_bir_lowering=False, num_devices=1)
    args = [nc.dram_tensor(name, a.shape, F32, kind="ExternalInput").ap() for name, a in arrays.items()]
    out = nc.dram_tensor("y_t", (P, KD, S), F32, kind="ExternalOutput").ap()
    build(nc, *args, out)
    r = run_bass_kernel_spmd(nc, [arrays], core_ids=[0])
    y = r.results[0]["y_t"]
    return np.ascontiguousarray(y.transpose(1, 0, 2).reshape(D, S).T)[None]
```
